# Optimizing a Trainium2 kernel written in Bass

```python
import jax, jax.numpy as jnp
from jax import lax
import numpy as np
import math

D_MODEL = 1024
BATCH = 1
SEQ = 256
DEPTH = 1

CHUNK = 64
N_META = 16
Q_BLOCK = 128
N_PAD = Q_BLOCK - N_META
PREFIX = N_PAD + N_META
MIX_WIDTH = D_MODEL
RET_HEADS = 4
RET_DV = (MIX_WIDTH // 2) // RET_HEADS
RET_DK = RET_DV // 2
FOX_HEADS = 8
FOX_DH = (MIX_WIDTH // 2) // FOX_HEADS
D_FF = 2816
CONV_W = 3
ROPE_BASE = 10000.0
EPS = 1e-6
NEG = -1e30

RET_QK = RET_HEADS * RET_DK
RET_V = RET_HEADS * RET_DV
FOX_W = FOX_HEADS * FOX_DH
SPLIT_POINTS = (RET_QK, 2 * RET_QK, 2 * RET_QK + RET_V, 2 * RET_QK + 2 * RET_V,
                2 * RET_QK + 2 * RET_V + FOX_W, 2 * RET_QK + 2 * RET_V + 2 * FOX_W,
                2 * RET_QK + 2 * RET_V + 3 * FOX_W)
IN_WIDTH = 2 * RET_QK + 2 * RET_V + 3 * FOX_W + FOX_HEADS


def rms_norm(x, g):
    xf = x.astype(jnp.float32)
    y = xf * lax.rsqrt(jnp.mean(xf * xf, axis=-1, keepdims=True) + EPS)
    return (y * g.astype(jnp.float32)).astype(x.dtype)

def rotary(x, pos):
    half = x.shape[-1] // 2
    inv = 1.0 / (ROPE_BASE ** (jnp.arange(half, dtype=jnp.float32) / half))
    ang = pos.astype(jnp.float32)[:, None] * inv[None, :]
    cos = jnp.cos(ang)[None, :, None, :]
    sin = jnp.sin(ang)[None, :, None, :]
    x1 = x[..., :half].astype(jnp.float32)
    x2 = x[..., half:].astype(jnp.float32)
    return jnp.concatenate([x1 * cos - x2 * sin, x1 * sin + x2 * cos], axis=-1)

def retention(q, k, v, valid):
    B, L, H, dk = q.shape
    dv = v.shape[-1]
    nc = L // CHUNK
    f32 = jnp.float32
    log_g = jnp.log1p(-jnp.exp2(-5.0 - jnp.arange(H, dtype=f32)))
    pos = jnp.arange(L)
    qr = rotary(q, pos)
    kr = rotary(k, pos) * (dk ** -0.5) * valid.astype(f32)[None, :, None, None]
    qc = qr.reshape(B, nc, CHUNK, H, dk)
    kc = kr.reshape(B, nc, CHUNK, H, dk)
    vc = v.astype(f32).reshape(B, nc, CHUNK, H, dv)
    n = jnp.arange(CHUNK, dtype=f32)
    d_intra = jnp.exp(jnp.abs(n[:, None] - n[None, :])[None] * log_g[:, None, None])
    s = jnp.einsum('bcnhd,bcmhd->bchnm', qc, kc) * d_intra[None, None]
    intra = jnp.einsum('bchnm,bcmhe->bcnhe', s, vc)
    w_k = jnp.exp((CHUNK - 1.0 - n)[:, None] * log_g[None, :])
    u = jnp.einsum('bcmhd,bcmhe->bchde', kc * w_k[None, None, :, :, None], vc)
    g_chunk = jnp.exp(CHUNK * log_g)[None, :, None, None]

    def step(r, u_i):
        return g_chunk * r + u_i, r

    _, r_prev = lax.scan(step, jnp.zeros((B, H, dk, dv), f32), jnp.moveaxis(u, 1, 0))
    r_prev = jnp.moveaxis(r_prev, 0, 1)
    w_q = jnp.exp((n + 1.0)[:, None] * log_g[None, :])
    inter = jnp.einsum('bcnhd,bchde->bcnhe', qc * w_q[None, None, :, :, None], r_prev)
    return (intra + inter).reshape(B, L, H, dv)

def forgetting_attention(q, k, v, log_f, valid):
    B, L, H, dh = q.shape
    f32 = jnp.float32
    scale = dh ** -0.5
    c = jnp.cumsum(log_f.astype(f32), axis=1).transpose(0, 2, 1)
    qf, kf, vf = q.astype(f32), k.astype(f32), v.astype(f32)
    pos = jnp.arange(L)
    outs = []
    for blk in range(L // Q_BLOCK):
        q0, q1 = blk * Q_BLOCK, (blk + 1) * Q_BLOCK
        logits = jnp.einsum('bqhd,bkhd->bhqk', qf[:, q0:q1], kf[:, :q1]) * scale
        bias = c[:, :, q0:q1, None] - c[:, :, None, :q1]
        mask = (pos[None, :q1] <= pos[q0:q1, None]) & valid[None, :q1]
        logits = jnp.where(mask[None, None], logits + bias, NEG)
        p = jax.nn.softmax(logits, axis=-1)
        outs.append(jnp.einsum('bhqk,bkhd->bqhd', p, vf[:, :q1]))
    return jnp.concatenate(outs, axis=1)

def hybrid_mixer(h, w_in, forget_b, ret_norm_g, w_out, valid):
    B, L, _ = h.shape
    proj = jnp.einsum('bld,de->ble', h, w_in)
    rq, rk, rv, rg, fq, fk, fv, ff = jnp.split(proj, SPLIT_POINTS, axis=-1)
    o_r = retention(rq.reshape(B, L, RET_HEADS, RET_DK), rk.reshape(B, L, RET_HEADS, RET_DK),
                    rv.reshape(B, L, RET_HEADS, RET_DV), valid)
    o_r = o_r * lax.rsqrt(jnp.mean(o_r * o_r, axis=-1, keepdims=True) + EPS)
    o_r = o_r.reshape(B, L, RET_V) * ret_norm_g.astype(jnp.float32) * jax.nn.silu(rg.astype(jnp.float32))
    log_f = jax.nn.log_sigmoid(ff.astype(jnp.float32) + forget_b.astype(jnp.float32))
    o_f = forgetting_attention(fq.reshape(B, L, FOX_HEADS, FOX_DH), fk.reshape(B, L, FOX_HEADS, FOX_DH),
                               fv.reshape(B, L, FOX_HEADS, FOX_DH), log_f, valid).reshape(B, L, FOX_W)
    mixed = jnp.concatenate([o_r, o_f], axis=-1).astype(h.dtype)
    return jnp.einsum('ble,ed->bld', mixed, w_out)

def conv_ffn(h, w_up, conv_w, conv_b, w_down, valid):
    L = h.shape[1]
    up = jnp.einsum('bld,df->blf', h, w_up)
    a, b = jnp.split(up, 2, axis=-1)
    a = a * valid.astype(a.dtype)[None, :, None]
    a_pad = jnp.pad(a, ((0, 0), (CONV_W - 1, 0), (0, 0)))
    acc = conv_b
    for j in range(CONV_W):
        acc = acc + a_pad[:, j:j + L] * conv_w[j]
    return jnp.einsum('blf,fd->bld', jax.nn.silu(acc) * b, w_down)

def first_inputs(seed: int = 0) -> dict:
    key = jax.random.key(seed)
    ks = jax.random.split(key, 13)
    f32 = jnp.float32
    return {
        "x": jax.random.normal(ks[0], (BATCH, SEQ, D_MODEL), f32),
        "meta_tokens": jax.random.normal(ks[1], (N_META, D_MODEL), f32),
        "attn_norm_g": 1.0 + 0.02 * jax.random.normal(ks[2], (DEPTH, D_MODEL), f32),
        "w_in": jax.random.normal(ks[3], (DEPTH, D_MODEL, IN_WIDTH), f32) * D_MODEL ** -0.5,
        "fox_forget_b": jax.random.uniform(ks[4], (DEPTH, FOX_HEADS), f32, 1.0, 5.0),
        "ret_norm_g": 1.0 + 0.02 * jax.random.normal(ks[5], (DEPTH, RET_V), f32),
        "w_out": jax.random.normal(ks[6], (DEPTH, MIX_WIDTH, D_MODEL), f32) * MIX_WIDTH ** -0.5,
        "ffn_norm_g": 1.0 + 0.02 * jax.random.normal(ks[7], (DEPTH, D_MODEL), f32),
        "w_up": jax.random.normal(ks[8], (DEPTH, D_MODEL, 2 * D_FF), f32) * D_MODEL ** -0.5,
        "conv_w": jax.random.normal(ks[9], (DEPTH, CONV_W, D_FF), f32) * CONV_W ** -0.5,
        "conv_b": 0.02 * jax.random.normal(ks[10], (DEPTH, D_FF), f32),
        "w_down": jax.random.normal(ks[11], (DEPTH, D_FF, D_MODEL), f32) * D_FF ** -0.5,
        "final_norm_g": 1.0 + 0.02 * jax.random.normal(ks[12], (D_MODEL,), f32),
    }

def first_block(x, meta_tokens, attn_norm_g, w_in, fox_forget_b, ret_norm_g, w_out,
              ffn_norm_g, w_up, conv_w, conv_b, w_down, final_norm_g):
    B = x.shape[0]
    pad = jnp.zeros((B, N_PAD, D_MODEL), x.dtype)
    meta = jnp.broadcast_to(meta_tokens.astype(x.dtype)[None], (B, N_META, D_MODEL))
    h = jnp.concatenate([pad, meta, x], axis=1)
    valid = jnp.arange(h.shape[1]) >= N_PAD
    for layer in range(DEPTH):
        h = h + hybrid_mixer(rms_norm(h, attn_norm_g[layer]), w_in[layer], fox_forget_b[layer],
                             ret_norm_g[layer], w_out[layer], valid)
        h = h + conv_ffn(rms_norm(h, ffn_norm_g[layer]), w_up[layer], conv_w[layer], conv_b[layer],
                         w_down[layer], valid)
    return rms_norm(h, final_norm_g)[:, PREFIX:]


DEPTH_2 = 2

SB_HEADS = 8
SB_HEAD_DIM = 64
SB_WIDTH = SB_HEADS * SB_HEAD_DIM
CONV_CH = D_MODEL // 2
CONV_K = 31
NORM_EPS = 1e-6
LN_EPS = 1e-5
IN_SIZES = [SB_WIDTH, SB_WIDTH, SB_WIDTH, CONV_CH, CONV_CH, D_MODEL, D_MODEL]
IN_SPLITS = [int(s) for s in np.cumsum(IN_SIZES)[:-1]]
IN_WIDTH_2 = int(sum(IN_SIZES))


def rmsnorm(x, g):
    xf = x.astype(jnp.float32)
    y = xf * lax.rsqrt(jnp.mean(xf * xf, axis=-1, keepdims=True) + NORM_EPS)
    return (y * g.astype(jnp.float32)).astype(x.dtype)

def layernorm(x, g, b):
    xf = x.astype(jnp.float32)
    mu = jnp.mean(xf, axis=-1, keepdims=True)
    var = jnp.mean(jnp.square(xf - mu), axis=-1, keepdims=True)
    y = (xf - mu) * lax.rsqrt(var + LN_EPS)
    return (y * g.astype(jnp.float32) + b.astype(jnp.float32)).astype(x.dtype)

def swiglu(x, w_gate, w_up, w_down):
    return (jax.nn.silu(x @ w_gate) * (x @ w_up)) @ w_down

def stick_breaking_attention(q, k, v):
    B, L, _ = q.shape
    Lp = ((L + Q_BLOCK - 1) // Q_BLOCK) * Q_BLOCK
    nb = Lp // Q_BLOCK

    def heads(a):
        a = a.reshape(B, L, SB_HEADS, SB_HEAD_DIM).transpose(0, 2, 1, 3).astype(jnp.float32)
        return jnp.pad(a, ((0, 0), (0, 0), (0, Lp - L), (0, 0)))

    qh, kh, vh = heads(q), heads(k), heads(v)
    scale = 1.0 / math.sqrt(SB_HEAD_DIM)
    q_blocks = qh.reshape(B, SB_HEADS, nb, Q_BLOCK, SB_HEAD_DIM).transpose(2, 0, 1, 3, 4)
    starts = jnp.arange(nb, dtype=jnp.int32) * Q_BLOCK
    key_pos = jnp.arange(Lp, dtype=jnp.int32)[None, :]

    def block(args):
        qb, start = args
        z = jnp.einsum('bhqd,bhkd->bhqk', qb, kh) * scale
        qpos = start + jnp.arange(Q_BLOCK, dtype=jnp.int32)[:, None]
        valid = key_pos < qpos
        log_keep = jnp.where(valid, jax.nn.log_sigmoid(-z), 0.0)
        after = lax.cumsum(log_keep, axis=3, reverse=True) - log_keep
        attn = jnp.where(valid, jnp.exp(jax.nn.log_sigmoid(z) + after), 0.0)
        return jnp.einsum('bhqk,bhkd->bhqd', attn, vh)

    out = lax.map(block, (q_blocks, starts))
    out = out.transpose(1, 2, 0, 3, 4).reshape(B, SB_HEADS, Lp, SB_HEAD_DIM)[:, :, :L]
    return out.transpose(0, 2, 1, 3).reshape(B, L, SB_WIDTH).astype(q.dtype)

def conformer_conv(a, b, conv_w, conv_b, ln_g, ln_b):
    u = a * jax.nn.sigmoid(b)
    y = lax.conv_general_dilated(
        u, conv_w[:, None, :].astype(u.dtype), window_strides=(1,),
        padding=[(CONV_K - 1, 0)],
        dimension_numbers=('NWC', 'WIO', 'NWC'), feature_group_count=CONV_CH)
    y = y + conv_b.astype(y.dtype)
    return jax.nn.silu(layernorm(y, ln_g, ln_b))

def hybrid_mixer_2(u, w_in, w_attn_out, conv_w, conv_b, conv_ln_g, conv_ln_b, w_conv_out, w_out):
    proj = u @ w_in
    q, k, v, a, b, g_sb, g_conv = jnp.split(proj, IN_SPLITS, axis=-1)
    y_sb = stick_breaking_attention(q, k, v) @ w_attn_out
    y_conv = conformer_conv(a, b, conv_w, conv_b, conv_ln_g, conv_ln_b) @ w_conv_out
    m = jax.nn.sigmoid(g_sb) * y_sb + jax.nn.sigmoid(g_conv) * y_conv
    return m @ w_out

def second_inputs(seed: int = 0) -> dict:
    key = jax.random.key(seed)
    ks = iter(jax.random.split(key, 32))

    def w(shape, fan_in, scale=1.0):
        return jax.random.normal(next(ks), shape, jnp.float32) * (scale * fan_in ** -0.5)

    def gain(shape):
        return 1.0 + 0.05 * jax.random.normal(next(ks), shape, jnp.float32)

    def bias(shape):
        return 0.02 * jax.random.normal(next(ks), shape, jnp.float32)

    L_ = DEPTH_2
    return {
        "x": jax.random.normal(next(ks), (BATCH, SEQ, D_MODEL), jnp.float32),
        "meta": jax.random.normal(next(ks), (N_META, D_MODEL), jnp.float32),
        "ffn1_norm": gain((L_, D_MODEL)),
        "ffn1_w_gate": w((L_, D_MODEL, D_FF), D_MODEL),
        "ffn1_w_up": w((L_, D_MODEL, D_FF), D_MODEL),
        "ffn1_w_down": w((L_, D_FF, D_MODEL), D_FF),
        "mix_norm": gain((L_, D_MODEL)),
        "w_in": w((L_, D_MODEL, IN_WIDTH_2), D_MODEL),
        "w_attn_out": w((L_, SB_WIDTH, D_MODEL), SB_WIDTH),
        "conv_w": w((L_, CONV_K, CONV_CH), CONV_K),
        "conv_b": bias((L_, CONV_CH)),
        "conv_ln_g": gain((L_, CONV_CH)),
        "conv_ln_b": bias((L_, CONV_CH)),
        "w_conv_out": w((L_, CONV_CH, D_MODEL), CONV_CH),
        "w_out": w((L_, D_MODEL, D_MODEL), D_MODEL),
        "ffn2_norm": gain((L_, D_MODEL)),
        "ffn2_w_gate": w((L_, D_MODEL, D_FF), D_MODEL),
        "ffn2_w_up": w((L_, D_MODEL, D_FF), D_MODEL),
        "ffn2_w_down": w((L_, D_FF, D_MODEL), D_FF),
        "final_norm": gain((D_MODEL,)),
    }

def second_block(x, meta, ffn1_norm, ffn1_w_gate, ffn1_w_up, ffn1_w_down, mix_norm, w_in,
              w_attn_out, conv_w, conv_b, conv_ln_g, conv_ln_b, w_conv_out, w_out,
              ffn2_norm, ffn2_w_gate, ffn2_w_up, ffn2_w_down, final_norm):
    B = x.shape[0]
    meta_b = jnp.broadcast_to(meta.astype(x.dtype)[None], (B, N_META, D_MODEL))
    h = jnp.concatenate([meta_b, x], axis=1)
    for l in range(DEPTH_2):
        h = h + 0.5 * swiglu(rmsnorm(h, ffn1_norm[l]), ffn1_w_gate[l], ffn1_w_up[l], ffn1_w_down[l])
        h = h + hybrid_mixer_2(rmsnorm(h, mix_norm[l]), w_in[l], w_attn_out[l], conv_w[l], conv_b[l],
                             conv_ln_g[l], conv_ln_b[l], w_conv_out[l], w_out[l])
        h = h + 0.5 * swiglu(rmsnorm(h, ffn2_norm[l]), ffn2_w_gate[l], ffn2_w_up[l], ffn2_w_down[l])
    h = rmsnorm(h, final_norm)
    return h[:, N_META:]


def setup_inputs(seed=0):
    out = dict(first_inputs(seed))
    for name, value in second_inputs(seed + 1).items():
        if name != "x":
            out[name + "_2"] = value
    return out


def reference(
    x, meta_tokens, attn_norm_g, w_in, fox_forget_b, ret_norm_g, w_out, ffn_norm_g, w_up,
    conv_w, conv_b, w_down, final_norm_g, meta_2, ffn1_norm_2, ffn1_w_gate_2, ffn1_w_up_2,
    ffn1_w_down_2, mix_norm_2, w_in_2, w_attn_out_2, conv_w_2, conv_b_2, conv_ln_g_2,
    conv_ln_b_2, w_conv_out_2, w_out_2, ffn2_norm_2, ffn2_w_gate_2, ffn2_w_up_2, ffn2_w_down_2,
    final_norm_2,
):
    x = first_block(
        x, meta_tokens, attn_norm_g, w_in, fox_forget_b, ret_norm_g, w_out, ffn_norm_g, w_up,
        conv_w, conv_b, w_down, final_norm_g,
    )
    return second_block(
        x, meta_2, ffn1_norm_2, ffn1_w_gate_2, ffn1_w_up_2, ffn1_w_down_2, mix_norm_2, w_in_2,
        w_attn_out_2, conv_w_2, conv_b_2, conv_ln_g_2, conv_ln_b_2, w_conv_out_2, w_out_2,
        ffn2_norm_2, ffn2_w_gate_2, ffn2_w_up_2, ffn2_w_down_2, final_norm_2,
    )


_drawn_inputs = setup_inputs


def setup_inputs(seed=0):
    import zlib

    import numpy as np

    out = dict(_drawn_inputs(seed))
    spreads = {}
    factors = {'ret_norm_g': 5.411,
     'ffn_norm_g': 3.419,
     'conv_b': 5.02,
     'conv_b_2': 3.576,
     'conv_ln_b_2': 6.626}
    for name, (base, spread) in spreads.items():
        noise = np.random.default_rng([zlib.crc32(name.encode()), seed]).standard_normal(out[name].shape)
        drawn = base * np.exp(spread * noise) if base else spread * noise
        out[name] = __import__('jax').numpy.asarray(drawn.astype(out[name].dtype))
    for name, factor in factors.items():
        out[name] = (out[name] * factor).astype(out[name].dtype)
    return out
```

```python
from contextlib import ExitStack

import numpy as np

import concourse.bass as bass
from concourse import mybir

F32 = mybir.dt.float32
F32R = mybir.dt.float32r
ALU = mybir.AluOpType
ACT = mybir.ActivationFunctionType

P = 128
D = 1024
DC = D // P
SEQ, META = 256, 16
T = META + SEQ
FF = 2816
FC = FF // P
LAYERS = 2
RET_H, RET_DK, RET_DV, CHUNK = 4, 64, 128, 64
FOX_H, FOX_DH = 8, 64
SB_H, SB_DH = 8, 64
CONV_W, CONV_K = 3, 31
CC = 4
PAD = 112
EPS, LN_EPS, NEG = 1e-6, 1e-5, -1e30
S8 = DC * P
HALF = FC // 2
S11 = HALF * P

BLK = [(0, 128), (128, 256), (256, 272)]
SB_AT = [0, 272, 416]
SBW = 432
FOX_AT = [0, 128, 384]
FOXW = 656
RET_FROM = [0, 80, 208]
RET_AT = [0, 272, 464]
RETW = 528

G_QKV1, G_WO1, G_UP1, G_DN1 = 0, 6, 8, 19
G_LAYER = 23
L_UPA, L_DNA, L_MIX, L_AC, L_WO, L_UPB, L_DNB = 0, 11, 15, 24, 26, 28, 39
PER_LAYER = 43
N_UP, N_DN, N_WO, N_QKV1, N_MIX, N_AC = 11, 4, 2, 6, 9, 2
W8_QKV1, W8_WO1, W8_UP1, W8_LAYER = 0, 24, 32, 76
W8_UPA, W8_MIX, W8_AC, W8_WO, W8_UPB = 0, 44, 80, 88, 96
W8_PER = 140
W11_LAYER, W11_PER = 16, 32
W8_TOTAL = W8_LAYER + LAYERS * W8_PER + 4

PRM_G = 0
PRM_RETG = 80
PRM_CW1 = PRM_RETG + RET_H
PRM_CB1 = PRM_CW1 + FC * CONV_W
PRM_CW2 = PRM_CB1 + FC
PRM_CB2 = PRM_CW2 + LAYERS * CC * CONV_K
PRM_LNG = PRM_CB2 + LAYERS * CC
PRM_LNB = PRM_LNG + LAYERS * CC
PRM_N = PRM_LNB + LAYERS * CC

o = 0
SC1 = {}
for name, n in [("later", T), ("mask", FOXW), ("dist", RETW), ("cos", T), ("sin", T), ("prob", FOXW),
                ("probT", SBW), ("fvT", 3 * 512), ("decay", 2 * T), ("wff", 64), ("fbias", 8), ("ff", 24),
                ("lf", 24), ("fe", 24), ("rtok", 4), ("mx", 4), ("nmx", 4), ("rsum", 4), ("rinv", 4)]:
    SC1[name] = (o, n)
    o += n
SC1_N = o
SC1_CONST = SC1["prob"][0]
o = 0
SC2 = {}
for name, n in [("kpad", CC * 384), ("u", CC * (CONV_K - 1 + T)), ("y", CC * T), ("soft", SBW),
                ("keep", SBW), ("attn", SBW)]:
    SC2[name] = (o, n)
    o += n
SC2_N = o
o = SC2["y"][0]
for name, n in [("gate", 2 * (T + 2)), ("act", 2 * T), ("up", T), ("prod", 2 * T)]:
    SC2[name] = (o, n)
    o += n
SC_N = max(SC1_N, SC2_N, o)

FQ, FK, FV, RQ, RK, RV, RG = 0, 4, 8, 12, 14, 16, 20
ROTQ, ROTK, RET_O, RET_VAR = 8, 10, 12, 0
VV, QQ, GSB, GCV = 0, 4, 8, 16


def build(nc, hT, meta2, w8, w11, wff, fbias, prm_d, cst1_d, cst_d, outT):
    ctx = ExitStack()
    with ctx:
        def sb(name, shape, dt=F32):
            return ctx.enter_context(nc.sbuf_tensor(name, shape, dt))

        def sem(name):
            return ctx.enter_context(nc.semaphore(name))

        raw = sb("raw", [P, 4, S11])
        whi = sb("whi", [P, 4, S11], F32R)
        wlo = sb("wlo", [P, 4, S11], F32R)
        h = sb("h", [P, DC, T])
        xh = sb("xh", [P, DC, T], F32R)
        xl = sb("xl", [P, DC, T], F32R)
        ah = sb("ah", [P, FC, T], F32R)
        al = sb("al", [P, FC, T], F32R)
        proj = sb("proj", [P, 24, T])
        vT = sb("vT", [P, 3, 512])
        scr = sb("scr", [P, SC_N])
        prm = sb("prm", [P, PRM_N])
        cst = sb("cst", [P, 3 * P + SBW])
        m2 = sb("m2", [P, DC, META])
        acc = sb("acc", [P, T])
        sq = sb("sq", [P, 2, T])
        rinv = sb("rinv", [P, T])
        warm = sb("warm", [P, 2])

        ones = cst[:, 0:P]
        ident = cst[:, P:2 * P]
        trige = cst[:, 2 * P:3 * P]
        unseen = cst[:, 3 * P:3 * P + SBW]

        def s1(name):
            a, n = SC1[name]
            return scr[:, a:a + n]

        def s2(name):
            a, n = SC2[name]
            return scr[:, a:a + n]

        later, fmask, dist, cos, sin = (s1(x) for x in ("later", "mask", "dist", "cos", "sin"))
        prob, probT, decay = s1("prob"), s1("probT"), s1("decay")
        fvT = s1("fvT").rearrange("p (b n) -> p b n", b=3)
        wff_s = s1("wff").rearrange("p (k n) -> p k n", k=DC)
        fb_s, ff_s, lf_s, fe_s = s1("fbias"), s1("ff"), s1("lf"), s1("fe")
        rtok, mx, nmx, rsum, rsinv = (s1(x) for x in ("rtok", "mx", "nmx", "rsum", "rinv"))
        kpad = s2("kpad").rearrange("p (c n) -> p c n", c=CC)
        u = s2("u").rearrange("p (c n) -> p c n", c=CC)
        y = s2("y").rearrange("p (c n) -> p c n", c=CC)
        soft, keep, attn = s2("soft"), s2("keep"), s2("attn")
        gate = s2("gate").rearrange("p (b n) -> p b n", b=2)
        actv = s2("act").rearrange("p (b n) -> p b n", b=2)
        upv = s2("up")
        prod = s2("prod").rearrange("p (b n) -> p b n", b=2)

        W = [ctx.enter_context(nc.psum_tensor(f"W{i}", [P, 512], F32)) for i in range(4)]
        X = [ctx.enter_context(nc.psum_tensor(f"X{i}", [P, 512], F32)) for i in range(4)]

        raw_landed = [sem(f"raw_landed{j}") for j in range(4)]
        hi_ready = [sem(f"hi_ready{j}") for j in range(4)]
        lo_ready = [sem(f"lo_ready{j}") for j in range(4)]
        mm_done = sem("mm_done")
        evac_done = sem("evac_done")
        xh_ready, xl_ready = sem("xh_ready"), sem("xl_ready")
        sq_ready, acc_done = sem("sq_ready"), sem("acc_done")
        acc_zero = sem("acc_zero")
        stat_mm, var_ready, sqrt_ready, r_ready = (sem(x) for x in ("stat_mm", "var_ready", "sqrt_ready", "r_ready"))
        conv_ready, act_ready = sem("conv_ready"), sem("act_ready")
        up_ready, prod_ready = sem("up_ready"), sem("prod_ready")
        ah_ready, al_ready = sem("ah_ready"), sem("al_ready")
        cv_step = sem("cv_step")
        zero_set = sem("zero_set")
        h_landed, prm_landed, cst_landed, c1_landed, m2_landed, ff_landed = (
            sem(x) for x in ("h_landed", "prm_landed", "cst_landed", "c1_landed", "m2_landed", "ff_landed"))
        ff_mm, ff_step, ff_var, ff_sqrt, ff_abs, ff_log, lf_ready = (
            sem(x) for x in ("ff_mm", "ff_step", "ff_var", "ff_sqrt", "ff_abs", "ff_log", "lf_ready"))
        vt_mm, vt_ready = sem("vt_mm"), sem("vt_ready")
        fl_mm, fl_max, fl_exp, fp_step, fp_ready, ft_mm, ft_ready, fo_mm, fo_hi, fo_lo, fl_step = (
            sem(x) for x in ("fl_mm", "fl_max", "fl_exp", "fp_step", "fp_ready", "ft_mm", "ft_ready", "fo_mm",
                             "fo_hi", "fo_lo", "fl_step"))
        rot_step, rot_ready = sem("rot_step"), sem("rot_ready")
        rs_mm, rd_ready, rs_ready, ro_mm, ro_copy, ro_sq, rv_mm, rvar_ready, rsqrt_ready, rn_step, rg_ready, ro_ready, ro_hi, ro_lo = (
            sem(x) for x in ("rs_mm", "rd_ready", "rs_ready", "ro_mm", "ro_copy", "ro_sq", "rv_mm", "rvar_ready",
                             "rsqrt_ready", "rn_step", "rg_ready", "ro_ready", "ro_hi", "ro_lo"))
        trans_done = sem("trans_done")
        glu_sig, u_ready, conv_step = (sem(x) for x in ("glu_sig", "u_ready", "conv_step"))
        v2_mm, v2_ready = sem("v2_mm"), sem("v2_ready")
        z_mm, soft_step, sp_step, keep_ready, cum_mm, arg_ready, attn_ready, o_mm, o_hi, o_lo = (
            sem(x) for x in ("z_mm", "soft_step", "sp_step", "keep_ready", "cum_mm", "arg_ready",
                             "attn_ready", "o_mm", "o_hi", "o_lo"))
        ln_step, ln_sum, ln_mm, ln_cent, ln_sq, ln_var, ln_sqrt, ln_rcp, ln_norm, ln_silu, s_hi, s_lo = (
            sem(x) for x in ("ln_step", "ln_sum", "ln_mm", "ln_cent", "ln_sq", "ln_var", "ln_sqrt", "ln_rcp", "ln_norm",
                             "ln_silu", "s_hi", "s_lo"))
        sig_ready, mix_ready, mix_hi, mix_lo = (
            sem(x) for x in ("sig_ready", "mix_ready", "mix_hi", "mix_lo"))
        out_ready, out_sent = sem("out_ready"), sem("out_sent")

        block = ctx.enter_context(nc.Block())

        POOL_ALL, SHARED = (0, 1, 2, 3), (0, 2)

        def ahead(j, own, nxt):
            return (0, 3, *own) if j == 0 else (1, j - 1, *nxt)

        K8A, K8S, K11 = (S8, POOL_ALL), (S8, SHARED), (S11, SHARED)

        @block.sync
        def _(sp):
            def load(g, src, j, cols, first=False):
                if not first:
                    sp.wait_ge(hi_ready[j], g)
                    sp.wait_ge(lo_ready[j], g)
                sp.dma_start(raw[:, j, 0:cols], src).then_inc(raw_landed[j], 16)

            def slab8(n):
                return w8[bass.ds(n, 1), :, :].rearrange("a p c -> p (a c)")

            def slab11(n):
                return w11[bass.ds(n, 1), :, :].rearrange("a p c -> p (a c)")

            def loads(n, g, slab, first_slab, cols):
                with sp.Fori(0, n) as i:
                    for j in range(4):
                        load(g + i, slab(first_slab + 4 * i + j), j, cols)

            sp.dma_start(h[:, :, :], hT).then_inc(h_landed, 16)
            sp.dma_start(prm[:, :], prm_d).then_inc(prm_landed, 16)
            for j in range(4):
                load(0, slab8(j), j, S8, first=True)
            sp.dma_start(cst[:, :], cst_d).then_inc(cst_landed, 16)
            sp.dma_start(wff_s, wff).then_inc(ff_landed, 16)
            sp.dma_start(fb_s, fbias).then_inc(ff_landed, 16)
            sp.dma_start(scr[:, 0:SC1_CONST], cst1_d).then_inc(c1_landed, 16)
            sp.dma_start(m2[:, :, :], meta2).then_inc(m2_landed, 16)
            loads(N_QKV1 - 1, 1, slab8, W8_QKV1 + 4, S8)
            loads(N_WO, G_WO1, slab8, W8_WO1, S8)
            loads(N_UP, G_UP1, slab8, W8_UP1, S8)
            loads(N_DN, G_DN1, slab11, 0, S11)
            with sp.Fori(0, LAYERS) as l:
                g, n8, n11 = G_LAYER + PER_LAYER * l, W8_LAYER + W8_PER * l, W11_LAYER + W11_PER * l
                loads(N_UP, g + L_UPA, slab8, n8 + W8_UPA, S8)
                loads(N_DN, g + L_DNA, slab11, n11, S11)
                loads(N_MIX, g + L_MIX, slab8, n8 + W8_MIX, S8)
                loads(N_AC, g + L_AC, slab8, n8 + W8_AC, S8)
                loads(N_WO, g + L_WO, slab8, n8 + W8_WO, S8)
                loads(N_UP, g + L_UPB, slab8, n8 + W8_UPB, S8)
                loads(N_DN, g + L_DNB, slab11, n11 + 16, S11)
            for j in range(3):
                load(G_LAYER + PER_LAYER * LAYERS, slab8(W8_TOTAL - 4 + j), j, S8)
            sp.wait_ge(out_ready, DC)
            sp.dma_start(outT, h[:, :, META:T]).then_inc(out_sent, 16)
            sp.wait_ge(out_sent, 16)

        @block.gpsimd
        def _(pool):
            def lo(g, j, cols):
                pool.wait_ge(hi_ready[j], g + 1)
                pool.tensor_tensor(wlo[:, j, 0:cols], raw[:, j, 0:cols], whi[:, j, 0:cols].bitcast(F32),
                                   ALU.subtract).then_inc(lo_ready[j], 1)

            def los(n, g, kind):
                cols, slots = kind
                with pool.Fori(0, n) as i:
                    for j in slots:
                        lo(g + i, j, cols)

            los(N_QKV1, G_QKV1, K8A)
            los(N_WO, G_WO1, K8S)
            los(N_UP, G_UP1, K8S)
            los(N_DN, G_DN1, K11)
            with pool.Fori(0, LAYERS) as l:
                g = G_LAYER + PER_LAYER * l
                los(N_UP, g + L_UPA, K8S)
                los(N_DN, g + L_DNA, K11)
                los(N_MIX, g + L_MIX, K8A)
                los(N_AC, g + L_AC, K8S)
                los(N_WO, g + L_WO, K8S)
                los(N_UP, g + L_UPB, K8S)
                los(N_DN, g + L_DNB, K11)

        @block.scalar
        def _(act):
            def hi(g, j, cols, first=False):
                act.wait_ge(raw_landed[j], 16 * g + 16)
                if not first:
                    act.wait_ge(mm_done, 4 * g + j - 3)
                act.activation(whi[:, j, 0:cols], raw[:, j, 0:cols], ACT.Copy).then_inc(hi_ready[j], 1)

            def hi_ahead(g, j, own, nxt):
                dg, slot, cols, _ = ahead(j, own, nxt)
                hi(g + dg, slot, cols, first=isinstance(g, int) and g + dg == 0)

            def warm_up(func):
                act.activation(warm[:, 1:2], warm[:, 0:1], func)

            def sqrt_stat(p):
                act.wait_ge(var_ready, p + 1)
                act.activation(rinv[:, :], rinv[:, :], ACT.Sqrt).then_inc(sqrt_ready, 1)

            def split_x(p, m):
                act.activation(xh[:, bass.ds(m, 1), :], h[:, bass.ds(m, 1), :], ACT.Copy,
                               scale=prm[:, bass.ds(PRM_G + 8 * p + m, 1)]).then_inc(xh_ready, 1)

            def square(p, m, b):
                act.activation(sq[:, b, :], h[:, bass.ds(m, 1), :], ACT.Square).then_inc(sq_ready, 1)

            def ffn_up(g, f, own, nxt, conv=False):
                def group(i, own, nxt):
                    for j in range(4):
                        b, c = j // 2, 2 * i + j // 2
                        hi_ahead(g + i, j, own, nxt)
                        if j % 2 == 0:
                            if conv:
                                act.wait_ge(conv_ready, c + 1)
                            else:
                                act.wait_ge(evac_done, 4 * (g + i) + j + 1)
                            act.activation(actv[:, b, :], gate[:, b, 2:T + 2], ACT.Silu).then_inc(act_ready, 1)
                        else:
                            act.wait_ge(prod_ready, FC * f + c + 1)
                            act.activation(ah[:, bass.ds(c, 1), :], prod[:, b, :], ACT.Copy).then_inc(ah_ready, 1)
                warm_up(ACT.Silu)
                with act.Fori(0, N_UP - 1) as i:
                    group(i, own, own)
                group(N_UP - 1, own, nxt)

            def residual_tail(g, p, m, b, n):
                act.wait_ge(acc_done, 8 * p + m - 1)
                act.wait_ge(evac_done, n)
                split_x(p, m)
                square(p, m, b)

            def ffn_down(g, p, nxt):
                def group(i, nxt):
                    for j in range(4):
                        hi_ahead(g + i, j, K11, nxt)
                        if j % 2:
                            residual_tail(g, p, 2 * i + j // 2, j // 2, 4 * (g + i) + j + 1)
                with act.Fori(0, N_DN - 1) as i:
                    group(i, K11)
                group(N_DN - 1, nxt)

            def out_proj(g, p):
                for i in range(N_WO):
                    for j in range(4):
                        hi_ahead(g + i, j, K8S, K8S)
                        residual_tail(g, p, 4 * i + j, j % 2, 4 * (g + i) + j + 1)

            act.wait_ge(h_landed, 16)
            act.wait_ge(prm_landed, 16)
            for j in range(3):
                hi(0, j, S8, first=True)
                split_x(0, j)
                if j >= 2:
                    act.wait_ge(acc_done, j - 1)
                square(0, j, j % 2)
            for m in range(3, DC):
                split_x(0, m)
                act.wait_ge(acc_done, m - 1)
                square(0, m, m % 2)

            def fox_exp(hd):
                act.wait_ge(fl_max, hd + 1)
                for b, (a, e) in enumerate(BLK):
                    r = e - a
                    w = FOX_AT[b + 1] - FOX_AT[b] if b < 2 else T
                    ins = act.activation(prob[0:r, FOX_AT[b]:FOX_AT[b] + w], prob[0:r, FOX_AT[b]:FOX_AT[b] + w],
                                         ACT.Exp, bias=nmx[0:r, b:b + 1], accum_out=rsum[0:r, b:b + 1])
                    ins.then_inc(fl_exp, 1)

            def fox_probT(hd):
                act.wait_ge(ft_mm, hd + 1)
                if hd >= 1:
                    act.wait_ge(fo_mm, hd)
                act.activation(probT[:, 0:416], X[2][:, 0:416], ACT.Copy).then_inc(ft_ready, 1)
                act.activation(probT[0:16, 416:SBW], X[2][0:16, 416:SBW], ACT.Copy).then_inc(ft_ready, 1)

            def fox_hi(c):
                act.wait_ge(fo_mm, 2 * c + 2)
                act.activation(ah[:, CC + c, :], X[3][:, 0:T], ACT.Copy).then_inc(fo_hi, 1)

            def ret_decay(hd):
                if hd >= 1:
                    act.wait_ge(ro_mm, hd)
                else:
                    act.wait_ge(rot_ready, 4)
                act.activation(decay[:, 0:RETW], dist, ACT.Exp,
                               scale=float(np.log1p(-2.0 ** (-5.0 - hd)))).then_inc(rd_ready, 1)

            for s in range(4 * N_QKV1):
                g, j = s // 4, s % 4
                hi_ahead(g, j, K8A, K8A if g < N_QKV1 - 1 else K8S)
                if s == 0:
                    sqrt_stat(0)
                if s == 5:
                    act.wait_ge(ff_var, 2)
                    act.activation(rtok[:, 0:3], rtok[:, 0:3], ACT.Sqrt).then_inc(ff_sqrt, 1)
                    act.wait_ge(ff_abs, 1)
                    act.activation(fe_s, fe_s, ACT.Exp, scale=-1.0).then_inc(ff_log, 1)
                    act.wait_ge(ff_log, 1)
                    act.activation(fe_s, fe_s, ACT.Ln, bias=1.0).then_inc(ff_log, 1)
                q = s - 12
                if 1 <= q <= 8:
                    fox_probT(q - 1)
                if q >= 3 and q % 2 and q <= 9:
                    fox_hi((q - 3) // 2)
                if 0 <= q < 8:
                    fox_exp(q)
                if q >= 9:
                    ret_decay(q - 9)
            ret_decay(3)
            act.wait_ge(evac_done, 4 * N_QKV1)
            act.activation(proj[:, RG:RG + 4, :], proj[:, RG:RG + 4, :], ACT.Silu).then_inc(rg_ready, 1)
            act.wait_ge(rvar_ready, RET_H)
            act.activation(proj[:, RET_VAR:RET_VAR + 4, :], proj[:, RET_VAR:RET_VAR + 4, :],
                           ACT.Sqrt).then_inc(rsqrt_ready, 1)
            for hd in range(RET_H):
                act.wait_ge(ro_ready, hd + 1)
                act.activation(ah[:, hd, :], proj[:, RET_O + hd, :], ACT.Copy).then_inc(ro_hi, 1)
            out_proj(G_WO1, 1)
            sqrt_stat(1)
            ffn_up(G_UP1, 0, K8S, K11, conv=True)
            ffn_down(G_DN1, 2, K8S)
            sqrt_stat(2)
            for m in range(DC):
                act.wait_ge(trans_done, m + 2)
                act.wait_ge(acc_done, 8 * 3 + m - 1)
                split_x(3, m)
                square(3, m, m % 2)

            def mixer(g, l, p):
                def soften(hd, bank):
                    n = 3 * (SB_H * l + hd)
                    act.wait_ge(z_mm, SB_H * l + hd + 1)
                    act.activation(soft, X[bank][:, 0:SBW], ACT.Abs).then_inc(soft_step, 1)
                    act.wait_ge(soft_step, n + 1)
                    act.activation(soft, soft, ACT.Exp, scale=-1.0).then_inc(soft_step, 1)
                    act.wait_ge(soft_step, n + 2)
                    act.activation(soft, soft, ACT.Ln, bias=1.0).then_inc(soft_step, 1)

                def weights(hd):
                    act.wait_ge(arg_ready, SB_H * l + hd + 1)
                    act.activation(attn, attn, ACT.Exp).then_inc(attn_ready, 1)

                def out_hi(c):
                    act.wait_ge(o_mm, SB_H * l + 2 * c + 2)
                    act.activation(ah[:, c, :], X[2][:, 0:T], ACT.Copy).then_inc(o_hi, 1)

                for i in range(2):
                    for j in range(4):
                        hi_ahead(g + i, j, K8A, K8A)
                        if j % 2:
                            c = 2 * i + j // 2
                            act.wait_ge(evac_done, 4 * (g + i) + j + 1)
                            act.activation(proj[:, 4 + c, :], proj[:, 4 + c, :], ACT.Sigmoid).then_inc(glu_sig, 1)
                for i in range(2, 5):
                    for j in range(4):
                        hi_ahead(g + i, j, K8A, K8A)
                for i in range(4):
                    for j in range(4):
                        hi_ahead(g + 5 + i, j, K8A, K8A if i < 3 else K8S)
                        if j == 0:
                            if i:
                                weights(2 * i - 1)
                                out_hi(i - 1)
                            soften(2 * i, 0)
                        elif j == 2:
                            weights(2 * i)
                        elif j == 3:
                            soften(2 * i + 1, 1)
                ga = g + N_MIX
                weights(SB_H - 1)
                out_hi(CC - 1)
                hi_ahead(ga, 0, K8S, K8S)
                act.wait_ge(evac_done, 4 * ga)
                act.activation(proj[:, GSB:GSB + DC, :], proj[:, GSB:GSB + DC, :], ACT.Sigmoid).then_inc(sig_ready, 1)
                for c in range(CC):
                    act.wait_ge(ln_cent, CC * l + c + 1)
                    act.activation(u[:, c, CONV_K - 1:], y[:, c, :], ACT.Square).then_inc(ln_sq, 1)
                act.activation(proj[:, GCV:GCV + DC, :], proj[:, GCV:GCV + DC, :], ACT.Sigmoid).then_inc(sig_ready, 1)
                hi_ahead(ga, 1, K8S, K8S)
                hi_ahead(ga, 2, K8S, K8S)
                act.wait_ge(ln_var, l + 1)
                act.activation(acc[:, :], acc[:, :], ACT.Sqrt).then_inc(ln_sqrt, 1)
                hi_ahead(ga, 3, K8S, K8S)
                for c in range(CC):
                    act.wait_ge(ln_norm, CC * l + c + 1)
                    act.activation(y[:, c, :], y[:, c, :], ACT.Silu, scale=prm[:, bass.ds(PRM_LNG + CC * l + c, 1)],
                                   bias=prm[:, bass.ds(PRM_LNB + CC * l + c, 1)]).then_inc(ln_silu, 1)
                    act.wait_ge(ln_silu, CC * l + c + 1)
                    act.activation(ah[:, CC + c, :], y[:, c, :], ACT.Copy).then_inc(s_hi, 1)
                for j in range(4):
                    hi_ahead(ga + 1, j, K8S, K8S)
                    for m in (2 * j, 2 * j + 1):
                        act.wait_ge(mix_ready, DC * l + m + 1)
                        act.activation(ah[:, DC + m, :], proj[:, GSB + m, :], ACT.Copy).then_inc(mix_hi, 1)
                out_proj(ga + N_AC, p)

            with act.Fori(0, LAYERS) as l:
                g, p = G_LAYER + PER_LAYER * l, 4 + 3 * l
                sqrt_stat(p - 1)
                ffn_up(g + L_UPA, 1 + 2 * l, K8S, K11)
                ffn_down(g + L_DNA, p, K8A)
                sqrt_stat(p)
                mixer(g + L_MIX, l, p + 1)
                sqrt_stat(p + 1)
                ffn_up(g + L_UPB, 2 + 2 * l, K8S, K11)
                ffn_down(g + L_DNB, p + 2, K8S)
            sqrt_stat(3 + 3 * LAYERS)

        @block.vector
        def _(dve):
            def lo_ahead(g, j, own, nxt):
                dg, slot, cols, pools = ahead(j, own, nxt)
                if slot not in pools:
                    dve.wait_ge(hi_ready[slot], g + dg + 1)
                    dve.tensor_tensor(wlo[:, slot, 0:cols], raw[:, slot, 0:cols], whi[:, slot, 0:cols].bitcast(F32),
                                      ALU.subtract).then_inc(lo_ready[slot], 1)

            def norm_factor(p):
                dve.wait_ge(stat_mm, p + 1)
                dve.tensor_scalar(rinv[:, :], X[3][:, 0:T], 1.0 / D, EPS, ALU.mult, ALU.add).then_inc(var_ready, 1)
                dve.wait_ge(sqrt_ready, p + 1)
                dve.reciprocal(rinv[:, :], rinv[:, :]).then_inc(r_ready, 1)

            def scaled(out, bank, n, cols=(0, T)):
                dve.wait_ge(mm_done, n)
                return dve.tensor_tensor(out, W[bank][:, cols[0]:cols[1]], rinv[:, :], ALU.mult)

            def split_tail(p, m, b):
                dve.wait_ge(xh_ready, 8 * p + m + 1)
                dve.scalar_tensor_tensor(xl[:, bass.ds(m, 1), :], h[:, bass.ds(m, 1), :],
                                         prm[:, bass.ds(PRM_G + 8 * p + m, 1)],
                                         xh[:, bass.ds(m, 1), :].bitcast(F32), ALU.mult, ALU.subtract).then_inc(xl_ready, 1)
                dve.wait_ge(sq_ready, 8 * p + m + 1)
                dve.wait_ge(acc_zero, p + 1)
                if isinstance(m, int) and isinstance(p, int) and 8 * p + m == 0:
                    pass
                else:
                    dve.wait_ge(acc_done, 8 * p + m)
                dve.tensor_tensor(acc[:, :], acc[:, :], sq[:, b, :], ALU.add).then_inc(acc_done, 1)

            def residual(p, m, b, bank, n, slabs, coef):
                dve.wait_ge(mm_done, n)
                dve.scalar_tensor_tensor(h[:, bass.ds(m, 1), :], W[bank][:, 0:T], coef, h[:, bass.ds(m, 1), :],
                                         ALU.mult, ALU.add).then_inc(evac_done, slabs)
                dve.wait_ge(evac_done, n)
                split_tail(p, m, b)

            def clear_sum():
                dve.memset(acc[:, :], 0.0).then_inc(acc_zero, 1)

            def ffn_up(g, f, p, own, nxt, conv=False):
                def group(i, own, nxt):
                    for j in range(4):
                        b, c = j // 2, 2 * i + j // 2
                        n = 4 * (g + i) + j + 1
                        lo_ahead(g + i, j, own, nxt)
                        if j == 0:
                            dve.wait_ge(r_ready, p + 1)
                        if j % 2 == 0 and not conv:
                            scaled(gate[:, b, 2:T + 2], j, n).then_inc(evac_done, 1)
                        elif j % 2 == 0:
                            scaled(gate[:, b, 2:T + 2], j, n).then_inc(evac_done, 1)
                            dve.wait_ge(evac_done, n)
                            w = [prm[:, bass.ds(PRM_CW1 + CONV_W * c + k, 1)] for k in range(CONV_W)]
                            dve.tensor_scalar(actv[:, b, :], gate[:, b, 0:T], w[0], prm[:, bass.ds(PRM_CB1 + c, 1)],
                                              ALU.mult, ALU.add).then_inc(cv_step, 1)
                            dve.wait_ge(cv_step, 2 * c + 1)
                            dve.scalar_tensor_tensor(actv[:, b, :], gate[:, b, 1:T + 1], w[1], actv[:, b, :],
                                                     ALU.mult, ALU.add).then_inc(cv_step, 1)
                            dve.wait_ge(cv_step, 2 * c + 2)
                            dve.scalar_tensor_tensor(gate[:, b, 2:T + 2], gate[:, b, 2:T + 2], w[2], actv[:, b, :],
                                                     ALU.mult, ALU.add).then_inc(conv_ready, 1)
                        else:
                            scaled(upv, j, n).then_inc(evac_done, 1)
                            dve.wait_ge(evac_done, n)
                            dve.wait_ge(act_ready, FC * f + c + 1)
                            dve.tensor_tensor(prod[:, b, :], actv[:, b, :], upv, ALU.mult).then_inc(prod_ready, 1)
                        if j >= 2:
                            cc = 2 * i + j - 2
                            dve.wait_ge(ah_ready, FC * f + cc + 1)
                            dve.tensor_tensor(al[:, bass.ds(cc, 1), :], prod[:, j - 2, :],
                                              ah[:, bass.ds(cc, 1), :].bitcast(F32), ALU.subtract).then_inc(al_ready, 1)
                with dve.Fori(0, N_UP - 1) as i:
                    group(i, own, own)
                group(N_UP - 1, own, nxt)

            def ffn_down(g, p, nxt, coef):
                def group(i, nxt):
                    for j in range(4):
                        lo_ahead(g + i, j, K11, nxt)
                        if j % 2:
                            residual(p, 2 * i + j // 2, j // 2, j - 1, 4 * (g + i) + j + 1, 2, coef)
                clear_sum()
                with dve.Fori(0, N_DN - 1) as i:
                    group(i, K11)
                group(N_DN - 1, nxt)

            def out_proj(g, p):
                clear_sum()
                for i in range(N_WO):
                    for j in range(4):
                        lo_ahead(g + i, j, K8S, K8S)
                        residual(p, 4 * i + j, j % 2, j, 4 * (g + i) + j + 1, 1, 1.0)

            dve.memset(warm[:, :], 0.0)
            clear_sum()
            dve.memset(rtok[:, :], 1.0).then_inc(zero_set, 1)
            dve.memset(ff_s, 0.0).then_inc(zero_set, 1)
            dve.memset(mx, 0.0).then_inc(zero_set, 1)
            dve.memset(rsum, 1.0).then_inc(zero_set, 1)
            dve.wait_ge(h_landed, 16)
            dve.wait_ge(prm_landed, 16)
            for m in range(DC):
                split_tail(0, m, m % 2)

            def rows(b):
                return BLK[b][1] - BLK[b][0]

            def forget_gates():
                dve.wait_ge(ff_mm, 1)
                dve.wait_ge(zero_set, 4)
                dve.wait_ge(ff_landed, 32)
                dve.tensor_scalar(rtok[:, 0:2], X[2][:, 32:34], 1.0 / D, EPS, ALU.mult, ALU.add).then_inc(ff_var, 1)
                dve.tensor_scalar(rtok[0:16, 2:3], X[2][0:16, 34:35], 1.0 / D, EPS, ALU.mult, ALU.add).then_inc(ff_var, 1)
                dve.wait_ge(ff_sqrt, 1)
                dve.reciprocal(rtok[:, 0:3], rtok[:, 0:3]).then_inc(ff_step, 1)
                dve.wait_ge(ff_step, 1)
                for b in range(3):
                    r = rows(b)
                    dve.scalar_tensor_tensor(ff_s[0:r, 8 * b:8 * b + 8], X[2][0:r, 8 * b:8 * b + 8], rtok[0:r, b:b + 1],
                                             fb_s[0:r, :], ALU.mult, ALU.add).then_inc(ff_step, 1)
                dve.wait_ge(ff_step, 4)
                dve.scalar_tensor_tensor(fe_s, ff_s, -1.0, ff_s, ALU.mult, ALU.max).then_inc(ff_abs, 1)
                dve.wait_ge(ff_log, 2)
                dve.scalar_tensor_tensor(lf_s, ff_s, 0.0, fe_s, ALU.min, ALU.subtract).then_inc(ff_step, 1)
                dve.wait_ge(ff_step, 5)
                dve.tensor_scalar(lf_s, lf_s, -1.0 / FOX_DH ** -0.5, None, ALU.mult).then_inc(lf_ready, 1)

            def fox_max(hd):
                dve.wait_ge(fl_mm, hd + 1)
                if hd == 0:
                    dve.wait_ge(c1_landed, 16)
                if hd >= 1:
                    dve.wait_ge(ft_mm, hd)
                for b in range(3):
                    r = rows(b)
                    w = FOX_AT[b + 1] - FOX_AT[b] if b < 2 else T
                    at = FOX_AT[b]
                    src = X[0][0:r, at:at + w] if b < 2 else X[1][0:r, 0:T]
                    dve.tensor_tensor_reduce(prob[0:r, at:at + w], src, fmask[0:r, at:at + w], FOX_DH ** -0.5, -3.0e38,
                                             ALU.add, ALU.max, mx[0:r, b:b + 1]).then_inc(fl_step, 1)
                dve.wait_ge(fl_step, 3 * hd + 3)
                dve.tensor_scalar(nmx[:, 0:3], mx[:, 0:3], -1.0, None, ALU.mult).then_inc(fl_max, 1)

            def fox_probs(hd):
                dve.wait_ge(fl_exp, 3 * hd + 3)
                dve.reciprocal(rsinv[:, 0:3], rsum[:, 0:3]).then_inc(fp_step, 1)
                dve.wait_ge(fp_step, hd + 1)
                for b in range(3):
                    r = rows(b)
                    w = FOX_AT[b + 1] - FOX_AT[b] if b < 2 else T
                    at = FOX_AT[b]
                    dve.tensor_scalar(prob[0:r, at:at + w], prob[0:r, at:at + w], rsinv[0:r, b:b + 1], None,
                                      ALU.mult).then_inc(fp_ready, 1)

            def fox_lo(c):
                dve.wait_ge(fo_hi, c + 1)
                dve.tensor_tensor(al[:, CC + c, :], X[3][:, 0:T], ah[:, CC + c, :].bitcast(F32),
                                  ALU.subtract).then_inc(fo_lo, 1)

            def values_on_tokens(dst, k, b, bank):
                dve.wait_ge(vt_mm, k + 1)
                dve.tensor_copy(dst[0:rows(b), b, :], X[bank][0:rows(b), :]).then_inc(vt_ready, 1)

            def rotary():
                dve.wait_ge(c1_landed, 16)
                n = 0
                for k, (src, dst) in enumerate(((RQ, ROTQ), (RK, ROTK))):
                    x1, x2 = proj[:, src, :], proj[:, src + 1, :]
                    t1, t2 = decay[:, 0:T], decay[:, T:2 * T]
                    for a, b, op, out in ((cos, sin, ALU.subtract, dst), (sin, cos, ALU.add, dst + 1)):
                        if n:
                            dve.wait_ge(rot_ready, n // 2)
                        dve.tensor_tensor(t1, x1, a, ALU.mult).then_inc(rot_step, 1)
                        dve.tensor_tensor(t2, x2, b, ALU.mult).then_inc(rot_step, 1)
                        n += 2
                        dve.wait_ge(rot_step, n)
                        dve.tensor_tensor(proj[:, out, :], t1, t2, op).then_inc(rot_ready, 1)

            def ret_weights(hd):
                dve.wait_ge(rs_mm, hd + 1)
                dve.wait_ge(rd_ready, hd + 1)
                for b in range(3):
                    r, w, at = rows(b), T - RET_FROM[b], RET_AT[b]
                    src = X[0][0:r, 0:w] if b == 0 else X[1][0:r, at - RET_AT[1]:at - RET_AT[1] + w]
                    dve.scalar_tensor_tensor(decay[0:r, at:at + w], src, RET_DK ** -0.5, decay[0:r, at:at + w],
                                             ALU.mult, ALU.mult).then_inc(rs_ready, 1)

            def ret_square(hd):
                dve.wait_ge(ro_mm, hd + 1)
                dve.tensor_copy(proj[:, RET_O + hd, :], X[2][:, 0:T]).then_inc(ro_copy, 1)
                dve.wait_ge(ro_copy, hd + 1)
                if hd >= 2:
                    dve.wait_ge(rv_mm, hd - 1)
                dve.tensor_tensor(sq[:, hd % 2, :], proj[:, RET_O + hd, :], proj[:, RET_O + hd, :],
                                  ALU.mult).then_inc(ro_sq, 1)

            def ret_var(hd):
                dve.wait_ge(rv_mm, hd + 1)
                dve.tensor_scalar(proj[:, RET_VAR + hd, :], X[3][:, 0:T], 1.0 / RET_DV, EPS, ALU.mult,
                                  ALU.add).then_inc(rvar_ready, 1)

            for s in range(4 * N_QKV1):
                g, j, q = s // 4, s % 4, s - 12
                if s == 0:
                    norm_factor(0)
                    dve.wait_ge(r_ready, 1)
                if 1 <= q <= 8:
                    fox_probs(q - 1)
                if q == 4:
                    dve.wait_ge(evac_done, 16)
                    rotary()
                lo_ahead(g, j, K8A, K8A if g < N_QKV1 - 1 else K8S)
                scaled(proj[:, s, :], j, s + 1).then_inc(evac_done, 1)
                if s == 5:
                    forget_gates()
                if s == 11:
                    dve.wait_ge(evac_done, 12)
                    for b, bank in enumerate((0, 1, 3)):
                        values_on_tokens(fvT, b, b, bank)
                if q >= 3 and q % 2 and q <= 9:
                    fox_lo((q - 3) // 2)
                if 0 <= q < 8:
                    fox_max(q)
                if q == 8:
                    values_on_tokens(vT, 3, 0, 0)
                    values_on_tokens(vT, 4, 1, 1)
                if q == 9:
                    values_on_tokens(vT, 5, 2, 0)
                    ret_weights(0)
                if q >= 10:
                    ret_square(q - 10)
                    ret_weights(q - 9)
                    ret_var(q - 10)
            ret_square(2)
            ret_weights(3)
            ret_var(2)
            ret_square(3)
            ret_var(3)
            dve.wait_ge(rsqrt_ready, 1)
            dve.reciprocal(proj[:, RET_VAR:RET_VAR + 4, :], proj[:, RET_VAR:RET_VAR + 4, :]).then_inc(rn_step, 1)
            dve.wait_ge(rn_step, 1)
            dve.wait_ge(rg_ready, 1)
            for hd in range(RET_H):
                dve.scalar_tensor_tensor(proj[:, RET_O + hd, :], proj[:, RET_O + hd, :], prm[:, PRM_RETG + hd:PRM_RETG + hd + 1],
                                         proj[:, RET_VAR + hd, :], ALU.mult, ALU.mult).then_inc(rn_step, 1)
            for hd in range(RET_H):
                dve.wait_ge(rn_step, 2 + hd)
                dve.tensor_tensor(proj[:, RET_O + hd, :], proj[:, RET_O + hd, :], proj[:, RG + hd, :],
                                  ALU.mult).then_inc(ro_ready, 1)
            for hd in range(RET_H):
                dve.wait_ge(ro_hi, hd + 1)
                dve.tensor_tensor(al[:, hd, :], proj[:, RET_O + hd, :], ah[:, hd, :].bitcast(F32),
                                  ALU.subtract).then_inc(ro_lo, 1)
            out_proj(G_WO1, 1)
            dve.memset(gate[:, :, 0:2], 0.0).then_inc(zero_set, 1)
            norm_factor(1)
            dve.wait_ge(zero_set, 5)
            ffn_up(G_UP1, 0, 1, K8S, K11, conv=True)
            ffn_down(G_DN1, 2, K8S, 1.0)

            norm_factor(2)
            dve.wait_ge(r_ready, 3)
            clear_sum()
            dve.wait_ge(m2_landed, 16)
            dve.tensor_copy(h[:, :, 0:META], m2[:, :, :]).then_inc(trans_done, 1)
            for m in range(DC):
                dve.scalar_tensor_tensor(h[:, m, META:T], h[:, m, META:T], prm[:, PRM_G + 16 + m:PRM_G + 17 + m],
                                         rinv[:, META:T], ALU.mult, ALU.mult).then_inc(trans_done, 1)
            for m in range(DC):
                dve.wait_ge(trans_done, m + 2)
                split_tail(3, m, m % 2)
            dve.memset(kpad[:, :, T:], 0.0).then_inc(zero_set, 1)
            dve.memset(u[:, :, 0:CONV_K - 1], 0.0).then_inc(zero_set, 1)
            dve.wait_ge(zero_set, 7)

            def mixer(g, l, p):
                def taps(k):
                    for c in range(CC):
                        w = prm[:, bass.ds(PRM_CW2 + CC * CONV_K * l + CONV_K * c + k, 1)]
                        n = CC * CONV_K * l + CC * k + c
                        if isinstance(k, int) and k == 0:
                            dve.wait_ge(u_ready, CC * l + c + 1)
                            dve.tensor_scalar(y[:, c, :], u[:, c, 0:T], w, prm[:, bass.ds(PRM_CB2 + CC * l + c, 1)],
                                              ALU.mult, ALU.add).then_inc(conv_step, 1)
                        else:
                            dve.wait_ge(conv_step, n - CC + 1)
                            dve.scalar_tensor_tensor(y[:, c, :], u[:, c, k:k + T], w, y[:, c, :], ALU.mult,
                                                     ALU.add).then_inc(conv_step, 1)

                def keeps(hd, bank):
                    n = SB_H * l + hd
                    dve.wait_ge(soft_step, 3 * n + 3)
                    dve.scalar_tensor_tensor(keep, X[bank][:, 0:SBW], 0.0, soft, ALU.max, ALU.add).then_inc(sp_step, 1)
                    dve.wait_ge(sp_step, n + 1)
                    dve.scalar_tensor_tensor(keep, unseen, 1.0, keep, ALU.subtract, ALU.mult).then_inc(keep_ready, 1)

                def arguments(hd, bank):
                    n = SB_H * l + hd
                    dve.wait_ge(cum_mm, n + 1)
                    dve.scalar_tensor_tensor(attn, unseen, NEG, X[bank][:, 0:SBW], ALU.mult, ALU.add).then_inc(arg_ready, 1)

                def out_lo(c):
                    dve.wait_ge(o_hi, CC * l + c + 1)
                    dve.tensor_tensor(al[:, c, :], X[2][:, 0:T], ah[:, c, :].bitcast(F32), ALU.subtract).then_inc(o_lo, 1)

                for i in range(2):
                    for j in range(4):
                        c, n = 2 * i + j // 2, 4 * (g + i) + j + 1
                        scaled(proj[:, c if j % 2 == 0 else 4 + c, :], j, n).then_inc(evac_done, 1)
                        if j % 2:
                            dve.wait_ge(glu_sig, CC * l + c + 1)
                            dve.tensor_tensor(u[:, c, CONV_K - 1:], proj[:, c, :], proj[:, 4 + c, :],
                                              ALU.mult).then_inc(u_ready, 1)
                for k in range(3):
                    taps(k)
                for i in range(2, 5):
                    for j in range(4):
                        n = 4 * (g + i) + j + 1
                        if i == 3:
                            dve.wait_ge(mm_done, n)
                            dve.scalar_tensor_tensor(proj[:, QQ + j, :], W[j][:, 0:T], SB_DH ** -0.5, rinv[:, :], ALU.mult,
                                                     ALU.mult).then_inc(evac_done, 1)
                        else:
                            scaled(proj[:, VV + j, :] if i == 2 else kpad[:, j, 0:T], j, n).then_inc(evac_done, 1)
                        taps(3 + 4 * (i - 2) + j)
                        if i == 3 and j < 3:
                            dve.wait_ge(v2_mm, 3 * l + j + 1)
                            dve.tensor_copy(vT[0:rows(j), j, :], X[1 + j][0:rows(j), :]).then_inc(v2_ready, 1)
                for i in range(4):
                    for j in range(4):
                        n = 4 * (g + 5 + i) + j + 1
                        if j == 0 and i:
                            arguments(2 * i - 1, 1)
                        elif j == 1:
                            keeps(2 * i, 0)
                        elif j == 2:
                            arguments(2 * i, 0)
                        elif j == 3:
                            keeps(2 * i + 1, 1)
                        lo_ahead(g + 5 + i, j, K8A, K8A if i < 3 else K8S)
                        scaled(proj[:, GSB + 4 * i + j, :], j, n).then_inc(evac_done, 1)
                        taps(15 + 4 * i + j)
                        if j == 0 and i:
                            out_lo(i - 1)
                ga = g + N_MIX
                arguments(SB_H - 1, 1)
                dve.wait_ge(conv_step, CC * CONV_K * (l + 1))
                dve.tensor_tensor(acc[:, :], y[:, 0, :], y[:, 1, :], ALU.add).then_inc(ln_step, 1)
                dve.tensor_tensor(sq[:, 0, :], y[:, 2, :], y[:, 3, :], ALU.add).then_inc(ln_step, 1)
                dve.wait_ge(ln_step, 5 * l + 2)
                dve.tensor_tensor(acc[:, :], acc[:, :], sq[:, 0, :], ALU.add).then_inc(ln_sum, 1)
                out_lo(CC - 1)
                lo_ahead(ga, 0, K8S, K8S)
                dve.wait_ge(ln_mm, 2 * l + 1)
                dve.tensor_scalar(sq[:, 1, :], X[3][:, 0:T], 1.0 / (CC * P), None, ALU.mult).then_inc(ln_step, 1)
                dve.wait_ge(ln_step, 5 * l + 3)
                for c in range(CC):
                    dve.tensor_tensor(y[:, c, :], y[:, c, :], sq[:, 1, :], ALU.subtract).then_inc(ln_cent, 1)

                def attn_gate(j):
                    for m in (2 * j, 2 * j + 1):
                        dve.wait_ge(mm_done, 4 * ga + j + 1)
                        dve.wait_ge(sig_ready, 2 * l + 1)
                        ins = dve.tensor_tensor(proj[:, GSB + m, :], W[m % 4][:, 0:T], proj[:, GSB + m, :], ALU.mult)
                    ins.then_inc(evac_done, 1)

                attn_gate(0)
                dve.wait_ge(ln_sq, CC * (l + 1))
                dve.tensor_tensor(acc[:, :], u[:, 0, CONV_K - 1:], u[:, 1, CONV_K - 1:], ALU.add).then_inc(ln_step, 1)
                dve.tensor_tensor(sq[:, 0, :], u[:, 2, CONV_K - 1:], u[:, 3, CONV_K - 1:], ALU.add).then_inc(ln_step, 1)
                dve.wait_ge(ln_step, 5 * l + 5)
                dve.tensor_tensor(acc[:, :], acc[:, :], sq[:, 0, :], ALU.add).then_inc(ln_sum, 1)
                lo_ahead(ga, 1, K8S, K8S)
                attn_gate(1)
                dve.wait_ge(ln_mm, 2 * l + 2)
                dve.tensor_scalar(acc[:, :], X[3][:, 0:T], 1.0 / (CC * P), LN_EPS, ALU.mult, ALU.add).then_inc(ln_var, 1)
                lo_ahead(ga, 2, K8S, K8S)
                attn_gate(2)
                dve.wait_ge(ln_sqrt, l + 1)
                dve.reciprocal(sq[:, 0, :], acc[:, :]).then_inc(ln_rcp, 1)
                dve.wait_ge(ln_rcp, l + 1)
                for c in range(CC):
                    dve.tensor_tensor(y[:, c, :], y[:, c, :], sq[:, 0, :], ALU.mult).then_inc(ln_norm, 1)
                lo_ahead(ga, 3, K8S, K8S)
                attn_gate(3)
                for c in range(CC):
                    dve.wait_ge(s_hi, CC * l + c + 1)
                    dve.tensor_tensor(al[:, CC + c, :], y[:, c, :], ah[:, CC + c, :].bitcast(F32),
                                      ALU.subtract).then_inc(s_lo, 1)
                gb = ga + 1
                for j in range(4):
                    lo_ahead(gb, j, K8S, K8S)
                    for m in (2 * j, 2 * j + 1):
                        dve.wait_ge(mm_done, 4 * gb + j + 1)
                        dve.wait_ge(sig_ready, 2 * l + 2)
                        ins = dve.tensor_tensor(proj[:, GCV + m, :], W[m % 4][:, 0:T], proj[:, GCV + m, :], ALU.mult)
                    ins.then_inc(evac_done, 1)
                    dve.wait_ge(evac_done, 4 * gb + j + 1)
                    for m in (2 * j, 2 * j + 1):
                        dve.tensor_tensor(proj[:, GSB + m, :], proj[:, GSB + m, :], proj[:, GCV + m, :],
                                          ALU.add).then_inc(mix_ready, 1)
                    for m in (2 * j, 2 * j + 1):
                        dve.wait_ge(mix_hi, DC * l + m + 1)
                        dve.tensor_tensor(al[:, DC + m, :], proj[:, GSB + m, :], ah[:, DC + m, :].bitcast(F32),
                                          ALU.subtract).then_inc(mix_lo, 1)
                out_proj(ga + N_AC, p)

            with dve.Fori(0, LAYERS) as l:
                g, p = G_LAYER + PER_LAYER * l, 4 + 3 * l
                norm_factor(p - 1)
                ffn_up(g + L_UPA, 1 + 2 * l, p - 1, K8S, K11)
                ffn_down(g + L_DNA, p, K8A, 0.5)
                norm_factor(p)
                dve.wait_ge(r_ready, p + 1)
                mixer(g + L_MIX, l, p + 1)
                norm_factor(p + 1)
                ffn_up(g + L_UPB, 2 + 2 * l, p + 1, K8S, K11)
                ffn_down(g + L_DNB, p + 2, K8S, 0.5)
            norm_factor(3 + 3 * LAYERS)
            dve.wait_ge(r_ready, 4 + 3 * LAYERS)
            for m in range(DC):
                dve.scalar_tensor_tensor(h[:, m, META:T], h[:, m, META:T], prm[:, PRM_G + 72 + m:PRM_G + 73 + m],
                                         rinv[:, META:T], ALU.mult, ALU.mult).then_inc(out_ready, 1)

        @block.tensor
        def _(pe):
            def emptied(n):
                if not (isinstance(n, int) and n <= 0):
                    pe.wait_ge(evac_done, n)

            def slab(g, j, rhs, out, at=0, start=True, stop=True, each=None):
                pe.wait_ge(lo_ready[j], g + 1)
                for k, (mh, ml) in enumerate(rhs):
                    if each is not None and k >= each[2]:
                        pe.wait_ge(each[0], each[1] + k - each[2] + 1)
                    w = slice((at + k) * P, (at + k + 1) * P)
                    pe.matmul(out, whi[:, j, w], mh, start=start and k == 0, stop=False, skip_group_check=True)
                    pe.matmul(out, whi[:, j, w], ml, start=False, stop=False, skip_group_check=True)
                    ins = pe.matmul(out, wlo[:, j, w], mh, start=False, stop=stop and k == len(rhs) - 1,
                                    skip_group_check=True)
                return ins

            X_RHS = [(xh[:, k, :], xl[:, k, :]) for k in range(DC)]
            A_RHS = [(ah[:, k, :], al[:, k, :]) for k in range(FC)]

            def stat(p):
                pe.wait_ge(acc_done, 8 * p + 8)
                pe.matmul(X[3][:, 0:T], ones, acc[:, :], start=True, stop=True, skip_group_check=True).then_inc(stat_mm, 1)

            def project(g, j, rhs, each=None, behind=3):
                emptied(4 * g + j - behind)
                slab(g, j, rhs, W[j][:, 0:T], each=each).then_inc(mm_done, 1)

            def ffn_up(g, p):
                for j in range(4):
                    project(g, j, X_RHS, each=(xl_ready, 8 * p, 0) if j == 0 else None)
                    if j == 0:
                        stat(p)
                with pe.Fori(1, N_UP) as i:
                    for j in range(4):
                        project(g + i, j, X_RHS)

            def ffn_down(g, f):
                def group(i, first=False):
                    for j in range(4):
                        half = j % 2
                        if half == 0:
                            emptied(4 * (g + i) + j - 3)
                        slab(g + i, j, A_RHS[half * HALF:(half + 1) * HALF], W[j - half][:, 0:T], start=half == 0,
                             stop=half == 1, each=(al_ready, FC * f + half * HALF, 0) if first and j < 2 else None).then_inc(mm_done, 1)
                group(0, first=True)
                with pe.Fori(1, N_DN) as i:
                    group(i)

            def out_proj(g, rhs, ready, behind=(3, 3, 3, 3)):
                for i in range(N_WO):
                    for j in range(4):
                        project(g + i, j, rhs, each=ready if i == 0 and j == 0 else None,
                                behind=3 if i else behind[j])

            def mm(out, lhsT, rhs, start):
                return pe.matmul(out, lhsT, rhs, start=start, stop=True, skip_group_check=True)

            def turn(out, c, src, b):
                a, e = BLK[b]
                if b < 2:
                    return pe.transpose(out[:, P * c:P * c + P], src[:, a:e], ident)
                return mm(out[0:16, P * c:P * c + P], src[:, a:e], ident, c == 0)

            def forget_logits():
                pe.wait_ge(ff_landed, 32)
                pe.wait_ge(acc_done, DC)
                first = True
                for b, (a, e) in enumerate(BLK):
                    r = e - a
                    for k in range(DC):
                        for part in (xh, xl):
                            mm(X[2][0:r, 8 * b:8 * b + 8], part[:, k, a:e].bitcast(F32), wff_s[:, k, :], first)
                            first = False
                    ins = mm(X[2][0:r, 32 + b:33 + b], acc[:, a:e], ones[:, 0:1], False)
                ins.then_inc(ff_mm, 1)

            def fox_logits(hd):
                c, p0 = hd // 2, 64 * (hd % 2)
                if hd == 0:
                    pe.wait_ge(vt_ready, 3)
                    pe.wait_ge(lf_ready, 1)
                    pe.wait_ge(c1_landed, 16)
                else:
                    pe.wait_ge(fl_max, hd)
                q, k = proj[p0:p0 + 64, FQ + c, :], proj[p0:p0 + 64, FK + c, :]

                def bias(out, b, m):
                    w = BLK[b][1]
                    for jb in range(b + 1):
                        a, e = BLK[jb]
                        lf = lf_s[0:e - a, 8 * jb + hd:8 * jb + hd + 1].to_broadcast([e - a, m])
                        ins = mm(out[:, a:w], lf, later[0:e - a, 0:w - a], False)
                    return ins

                mm(X[0][:, 0:128], q[:, 0:128], k[:, 0:128], True)
                mm(X[0][:, 128:384], q[:, 128:256], k[:, 0:256], False)
                bias(X[0][:, 0:128], 0, P)
                bias(X[0][:, 128:384], 1, P)
                mm(X[1][0:16, 0:T], q[:, 256:T], k[:, 0:T], True)
                bias(X[1][0:16, 0:T], 2, 16).then_inc(fl_mm, 1)

            def fox_turn(hd):
                pe.wait_ge(fp_ready, 3 * hd + 3)
                if hd:
                    pe.wait_ge(ft_ready, 2 * hd)
                pe.transpose(X[2][:, 0:128], prob[:, 0:128], ident)
                pe.transpose(X[2][:, 128:256], prob[:, 128:256], ident)
                pe.transpose(X[2][:, 256:272], prob[0:16, 384:512], ident[0:16, 0:16])
                pe.transpose(X[2][:, 272:400], prob[:, 256:384], ident)
                pe.transpose(X[2][:, 400:416], prob[0:16, 512:640], ident[0:16, 0:16])
                mm(X[2][0:16, 416:432], prob[0:16, 640:656], ident[0:16, 0:16], True).then_inc(ft_mm, 1)

            def fox_values(hd):
                c, p0 = hd // 2, 64 * (hd % 2)
                pe.wait_ge(ft_ready, 2 * hd + 2)
                if c and not p0:
                    pe.wait_ge(fo_lo, c)
                for b in range(3):
                    r = BLK[b][1] - BLK[b][0]
                    ins = mm(X[3][p0:p0 + 64, BLK[b][0]:T], fvT[0:r, b, 64 * hd:64 * hd + 64],
                             probT[0:r, SB_AT[b]:SB_AT[b] + T - BLK[b][0]], b == 0)
                ins.then_inc(fo_mm, 1)

            def ret_scores(hd):
                pe.wait_ge(rot_ready, 4)
                if hd == 0:
                    pe.wait_ge(vt_ready, 6)
                else:
                    pe.wait_ge(rs_ready, 3 * hd)
                p0 = 32 * hd
                for b in range(3):
                    a, e = BLK[b]
                    w = T - RET_FROM[b]
                    at = RET_AT[b] - (RET_AT[1] if b else 0)
                    for half in range(2):
                        ins = mm(X[min(b, 1)][0:e - a, at:at + w], proj[p0:p0 + 32, ROTK + half, a:e],
                                 proj[p0:p0 + 32, ROTQ + half, RET_FROM[b]:T], b < 2 and half == 0)
                ins.then_inc(rs_mm, 1)

            def ret_values(hd):
                pe.wait_ge(rs_ready, 3 * hd + 3)
                if hd == 0:
                    pe.wait_ge(ft_ready, 2 * FOX_H)
                else:
                    pe.wait_ge(ro_copy, hd)
                for b in range(3):
                    r = BLK[b][1] - BLK[b][0]
                    ins = mm(X[2][:, RET_FROM[b]:T], vT[0:r, b, P * hd:P * hd + P],
                             decay[0:r, RET_AT[b]:RET_AT[b] + T - RET_FROM[b]], b == 0)
                ins.then_inc(ro_mm, 1)

            def ret_sums(hd):
                pe.wait_ge(ro_sq, hd + 1)
                if hd == 0:
                    pe.wait_ge(fo_lo, CC)
                else:
                    pe.wait_ge(rvar_ready, hd)
                mm(X[3][:, 0:T], ones, sq[:, hd % 2, :], True).then_inc(rv_mm, 1)

            pe.wait_ge(cst_landed, 16)
            for s in range(4 * N_QKV1):
                g, j, q = s // 4, s % 4, s - 12
                project(g, j, X_RHS, each=(xl_ready, 0, 0) if s == 0 else None)
                if s == 0:
                    stat(0)
                if s == 3:
                    forget_logits()
                if s == 11:
                    pe.wait_ge(evac_done, 12)
                    pe.wait_ge(var_ready, 1)
                    for b, bank in enumerate((0, 1, 3)):
                        for c in range(CC):
                            ins = turn(X[bank], c, proj[:, FV + c, :], b)
                        ins.then_inc(vt_mm, 1)
                if 0 <= q - 2 < 8:
                    fox_values(q - 2)
                if 0 <= q - 1 < 8:
                    fox_turn(q - 1)
                if 0 <= q < 8:
                    fox_logits(q)
                if q in (8, 9):
                    pe.wait_ge(fl_max, FOX_H)
                    pe.wait_ge(evac_done, 20)
                    if q == 9:
                        pe.wait_ge(vt_ready, 4)
                    for b, bank in ((0, 0), (1, 1)) if q == 8 else ((2, 0),):
                        for c in range(CC):
                            ins = turn(X[bank], c, proj[:, RV + c, :], b)
                        ins.then_inc(vt_mm, 1)
                if q >= 10:
                    ret_values(q - 10)
                if q >= 9:
                    ret_scores(q - 9)
                if q >= 10:
                    ret_sums(q - 10)
            ret_values(2)
            ret_scores(3)
            ret_sums(2)
            ret_values(3)
            ret_sums(3)
            pe.wait_ge(fo_lo, CC)
            out_proj(G_WO1, A_RHS[CC:DC] + A_RHS[0:CC], (ro_lo, 0, CC))
            ffn_up(G_UP1, 1)
            ffn_down(G_DN1, 0)
            stat(2)

            def mixer(g, l):
                def scores(hd):
                    c, p0, bank = hd // 2, 64 * (hd % 2), hd % 2
                    if hd == 0:
                        pe.wait_ge(evac_done, 4 * (g + 5))
                    elif hd == 1:
                        pe.wait_ge(v2_ready, 3 * l + 3)
                    else:
                        pe.wait_ge(arg_ready, SB_H * l + hd - 1)
                    for b in range(3):
                        a, w = P * b, T - P * b
                        ins = mm(X[bank][:, SB_AT[b]:SB_AT[b] + w], kpad[p0:p0 + 64, c, a:a + P],
                                 proj[p0:p0 + 64, QQ + c, a:T], b == 0)
                    ins.then_inc(z_mm, 1)

                def sums(hd):
                    bank = hd % 2
                    pe.wait_ge(keep_ready, SB_H * l + hd + 1)
                    for b in range(3):
                        for jb in range(b, 3):
                            r = BLK[jb][1] - BLK[jb][0]
                            w = T - P * jb
                            ins = mm(X[bank][:, SB_AT[b] + P * (jb - b):SB_AT[b] + P * (jb - b) + w],
                                     (trige if jb == b else ones)[0:r, :], keep[0:r, SB_AT[jb]:SB_AT[jb] + w], False)
                    ins.then_inc(cum_mm, 1)

                def values(hd):
                    c, p0 = hd // 2, 64 * (hd % 2)
                    pe.wait_ge(attn_ready, SB_H * l + hd + 1)
                    if hd == 0:
                        pe.wait_ge(v2_ready, 3 * l + 3)
                    elif p0 == 0:
                        pe.wait_ge(o_lo, CC * l + c)
                    for b in range(3):
                        r = BLK[b][1] - BLK[b][0]
                        ins = mm(X[2][p0:p0 + 64, P * b:T], vT[0:r, b, 64 * hd:64 * hd + 64],
                                 attn[0:r, SB_AT[b]:SB_AT[b] + T - P * b], b == 0)
                    ins.then_inc(o_mm, 1)

                for i in range(5):
                    for j in range(4):
                        project(g + i, j, X_RHS, each=(xl_ready, 8 * (4 + 3 * l), 0) if i == 0 and j == 0 else None)
                        if i == 0 and j == 0:
                            stat(4 + 3 * l)
                        if i == 3 and j == 0:
                            pe.wait_ge(evac_done, 4 * (g + 3))
                            for b in range(3):
                                for c in range(CC):
                                    ins = turn(X[1 + b], c, proj[:, VV + c, :], b)
                                ins.then_inc(v2_mm, 1)
                for i in range(4):
                    project(g + 5 + i, 0, X_RHS)
                    if i:
                        values(2 * i - 1)
                    scores(2 * i)
                    project(g + 5 + i, 1, X_RHS)
                    sums(2 * i)
                    project(g + 5 + i, 2, X_RHS)
                    values(2 * i)
                    scores(2 * i + 1)
                    project(g + 5 + i, 3, X_RHS)
                    sums(2 * i + 1)
                ga = g + N_MIX
                values(SB_H - 1)

                def channel_sums(k):
                    pe.wait_ge(ln_sum, 2 * l + k)
                    mm(X[3][:, 0:T], ones, acc[:, :], True).then_inc(ln_mm, 1)

                def branch(ga, j, rhs):
                    emptied(4 * ga + j - 1)
                    for half in range(2):
                        ins = slab(ga, j, rhs, W[(2 * j + half) % 4][:, 0:T], at=CC * half)
                    ins.then_inc(mm_done, 1)

                channel_sums(1)
                pe.wait_ge(o_lo, CC * l + CC)
                for j in range(4):
                    branch(ga, j, A_RHS[0:CC])
                    if j == 1:
                        channel_sums(2)
                pe.wait_ge(s_lo, CC * l + CC)
                for j in range(4):
                    branch(ga + 1, j, A_RHS[CC:2 * CC])
                out_proj(ga + N_AC, A_RHS[DC:2 * DC], (mix_lo, DC * l, 0), behind=(1, 2, 2, 3))

            with pe.Fori(0, LAYERS) as l:
                g, p = G_LAYER + PER_LAYER * l, 4 + 3 * l
                ffn_up(g + L_UPA, p - 1)
                ffn_down(g + L_DNA, 1 + 2 * l)
                mixer(g + L_MIX, l)
                ffn_up(g + L_UPB, p + 1)
                ffn_down(g + L_DNB, 2 + 2 * l)
            stat(3 + 3 * LAYERS)


def tiles(w, cols):
    k = w.shape[0] // P
    return w[:, cols].reshape(k, P, P).transpose(1, 0, 2).reshape(P, k * P)


def chunk_cols(start, n):
    return [np.arange(start + P * c, start + P * c + P) for c in range(n)]


def interleaved(a, b):
    return [x for pair in zip(a, b) for x in pair]


def half_heads(start):
    head = np.arange(RET_H)[:, None] * RET_DK + np.arange(RET_DK // 2)[None, :]
    return [start + head.reshape(-1), start + RET_DK // 2 + head.reshape(-1)]


def down_slabs(w):
    return [tiles(w[half * HALF * P:(half + 1) * HALF * P], c) for c in chunk_cols(0, DC) for half in range(2)]


def branch_slabs(w):
    cols = chunk_cols(0, DC)
    return [np.concatenate([tiles(w, cols[2 * j]), tiles(w, cols[2 * j + 1])], 1) for j in range(4)]


def chunked(v):
    return np.asarray(v).reshape(-1, P).T


def constants():
    i = np.arange(P)
    ident = np.eye(P)
    trige = (i[:, None] >= i[None, :])
    unseen = np.ones((P, SBW))
    for b, (a, e) in enumerate(BLK):
        key, query = P * b + i[:, None], np.arange(P * b, T)[None, :]
        unseen[:, SB_AT[b]:SB_AT[b] + T - P * b] = ~((key < query) & (key < T))
    every = np.concatenate([np.ones((P, P)), ident, trige, unseen], 1)
    later = (i[:, None] <= np.arange(T)[None, :])
    mask = np.zeros((P, FOXW))
    for b, (a, e) in enumerate(BLK):
        w = FOX_AT[b + 1] - FOX_AT[b] if b < 2 else T
        mask[:, FOX_AT[b]:FOX_AT[b] + w] = np.where(np.arange(w)[None, :] <= a + i[:, None], 0.0, NEG * FOX_DH ** 0.5)
    dist = np.full((P, RETW), 1e5)
    for b, (a, e) in enumerate(BLK):
        s, t = a + i[:, None], np.arange(RET_FROM[b], T)[None, :]
        seen = ((s + PAD) // CHUNK <= (t + PAD) // CHUNK) & (s < T)
        dist[:, RET_AT[b]:RET_AT[b] + T - RET_FROM[b]] = np.where(seen, np.abs(t - s), 1e5)
    half = RET_DK // 2
    inv = 1.0 / (np.float32(10000.0) ** (np.arange(half, dtype=np.float32) / np.float32(half)))
    ang = (np.arange(T, dtype=np.float32)[None, :] + np.float32(PAD)) * inv.astype(np.float32)[:, None]
    ang = np.tile(ang, (RET_H, 1)).astype(np.float32)
    first = np.concatenate([later, mask, dist, np.cos(ang), np.sin(ang)], 1)
    return first.astype(np.float32), every.astype(np.float32)


def kernel(**inputs):
    import concourse.bacc as bacc
    from concourse.bass_utils import run_bass_kernel_spmd

    a = {k: np.asarray(v) for k, v in inputs.items()}
    w_in = a["w_in"][0]
    at = np.cumsum([0, 256, 256, 512, 512, 512, 512, 512])
    order = chunk_cols(at[4], 12) + half_heads(at[0]) + half_heads(at[1]) + chunk_cols(at[2], 8)
    s8 = [tiles(w_in, c) for c in order]
    w_out = np.roll(a["w_out"][0], D // 2, axis=0)
    s8 += [tiles(w_out, c) for c in chunk_cols(0, DC)]
    s8 += [tiles(a["w_up"][0], c) for c in interleaved(chunk_cols(0, FC), chunk_cols(FF, FC))]
    s11 = down_slabs(a["w_down"][0])
    for l in range(LAYERS):
        for f in ("ffn1", "ffn2"):
            up = [tiles(w, c) for c in chunk_cols(0, FC) for w in (a[f + "_w_gate_2"][l], a[f + "_w_up_2"][l])]
            if f == "ffn2":
                w = a["w_in_2"][l]
                cols = (interleaved(chunk_cols(1536, 4), chunk_cols(2048, 4)) + chunk_cols(1024, 4) + chunk_cols(0, 8)
                        + chunk_cols(2560, 16))
                s8 += [tiles(w, c) for c in cols]
                s8 += branch_slabs(a["w_attn_out_2"][l]) + branch_slabs(a["w_conv_out_2"][l])
                s8 += [tiles(a["w_out_2"][l], c) for c in chunk_cols(0, DC)]
            s8 += up
            s11 += down_slabs(a[f + "_w_down_2"][l])
    s8 += s8[:4]
    gains = [a["attn_norm_g"][0], a["ffn_norm_g"][0], a["final_norm_g"]]
    for l in range(LAYERS):
        gains += [a["ffn1_norm_2"][l], a["mix_norm_2"][l], a["ffn2_norm_2"][l]]
    gains.append(a["final_norm_2"])
    prm = [chunked(g) for g in gains] + [chunked(a["ret_norm_g"][0])]
    prm.append(a["conv_w"][0].reshape(CONV_W, FC, P).transpose(2, 1, 0).reshape(P, FC * CONV_W))
    prm.append(chunked(a["conv_b"][0]))
    prm += [a["conv_w_2"][l].reshape(CONV_K, CC, P).transpose(2, 1, 0).reshape(P, CC * CONV_K) for l in range(LAYERS)]
    prm += [chunked(a[n]) for n in ("conv_b_2", "conv_ln_g_2", "conv_ln_b_2")]
    first, every = constants()
    arrays = {
        "hT": np.concatenate([a["meta_tokens"], a["x"][0]], 0).T.reshape(DC, P, T).transpose(1, 0, 2),
        "meta2": a["meta_2"].T.reshape(DC, P, META).transpose(1, 0, 2),
        "w8": np.stack(s8),
        "w11": np.stack(s11),
        "wff": w_in[:, at[7]:].reshape(DC, P, 8).transpose(1, 0, 2),
        "fbias": np.broadcast_to(a["fox_forget_b"], (P, 8)),
        "prm": np.concatenate(prm, 1),
        "cst1": first,
        "cst": every,
    }
    arrays = {k: np.ascontiguousarray(v) for k, v in arrays.items()}

    nc = bacc.Bacc("TRN2", target_bir_lowering=False, num_devices=1)
    args = [nc.dram_tensor("in_" + k, v.shape, mybir.dt.from_np(v.dtype), kind="ExternalInput").ap()
            for k, v in arrays.items()]
    out = nc.dram_tensor("out_0", (P, DC, SEQ), F32, kind="ExternalOutput").ap()
    build(nc, *args, out)
    r = run_bass_kernel_spmd(nc, [{"in_" + k: v for k, v in arrays.items()}], core_ids=[0])
    got = r.results[0]["out_0"]
    return got.transpose(2, 1, 0).reshape(1, SEQ, D)
```

```python
from contextlib import ExitStack

import numpy as np

import concourse.bass as bass
from concourse import mybir

F32 = mybir.dt.float32
F32R = mybir.dt.float32r
ALU = mybir.AluOpType
ACT = mybir.ActivationFunctionType

P = 128
D = 1024
DC = D // P
SEQ, META = 256, 16
T = META + SEQ
FF = 2816
FC = FF // P
LAYERS = 2
RET_H, RET_DK, RET_DV, CHUNK = 4, 64, 128, 64
FOX_H, FOX_DH = 8, 64
SB_H, SB_DH = 8, 64
CONV_W, CONV_K = 3, 31
CC = 4
T_A, T_B = META - CONV_W + 1, META
PAD = 112
EPS, LN_EPS, NEG = 1e-6, 1e-5, -1e30
S8 = DC * P
HALF = FC // 2
S11 = HALF * P

BLK = [(0, 128), (128, 256), (256, 272)]
SB_AT = [0, 272, 416]
SBW = 432
FOX_AT = [0, 128, 384]
FOXW = 656
FOX_BLK = [(128, 0, 128), (128, 128, 256), (16, 384, 272)]
RET_FROM = [0, 80, 208]
RET_AT = [0, 272, 464]
RETW = 528

G_QKV1, G_WO1, G_UP1, G_DN1 = 0, 6, 8, 19
G_LAYER = 23
L_UPA, L_DNA, L_MIX, L_AC, L_WO, L_UPB, L_DNB = 0, 11, 15, 24, 26, 28, 39
PER_LAYER = 43
N_UP, N_DN, N_WO, N_QKV1, N_MIX, N_AC = 11, 4, 2, 6, 9, 2
W8_QKV1, W8_WO1, W8_UP1, W8_LAYER = 0, 24, 32, 76
W8_UPA, W8_MIX, W8_AC, W8_WO, W8_UPB = 0, 44, 80, 88, 96
W8_PER = 140
W11_LAYER, W11_PER = 16, 32
W8_TOTAL = W8_LAYER + LAYERS * W8_PER + 4

PRM_G = 0
PRM_RETG = 80
PRM_CW1 = PRM_RETG + RET_H
PRM_CB1 = PRM_CW1 + FC * CONV_W
PRM_CW2 = PRM_CB1 + FC
PRM_CB2 = PRM_CW2 + LAYERS * CC * CONV_K
PRM_LNG = PRM_CB2 + LAYERS * CC
PRM_LNB = PRM_LNG + LAYERS * CC
PRM_N = PRM_LNB + LAYERS * CC

o = 0
SC1 = {}
for name, n in [("later", T), ("mask", FOXW), ("dist", RETW), ("cos", T), ("sin", T), ("prob", 2 * FOXW),
                ("probT", SBW), ("decay", 2 * RETW), ("csum", T), ("wff", DC * FOX_H), ("wffg", DC * FOX_H),
                ("fbias", 1), ("lf", 3 * FOX_H), ("mx", 8), ("nmx", 8), ("rsum", 8), ("rinv", 8)]:
    SC1[name] = (o, n)
    o += n
SC1_N = o
SC1["ff"] = (SC1["decay"][0], T)
SC1["fe"] = (SC1["decay"][0] + T, T)
SC1_CONST = SC1["prob"][0]
o = 0
SC2 = {}
for name, n in [("kpad", CC * 384), ("u", CC * (CONV_K - 1 + T)), ("y", CC * T), ("soft", SBW),
                ("keep", SBW), ("attn", SBW)]:
    SC2[name] = (o, n)
    o += n
SC2_N = o
o = SC2["y"][0]
for name, n in [("gate", 2 * (T + 2)), ("act", 2 * T), ("up", T), ("prod", 2 * T)]:
    SC2[name] = (o, n)
    o += n
SC_N = max(SC1_N, SC2_N, o)

G_GLU, G_V, G_QK = 8, 12, 20
SB_FROM = 14
LN_FROM = 27


def tap_plan():
    plan, done, last, n = [], [0] * CC, [None] * CC, 0
    for s in range(4 * N_MIX):
        room = 0 if s < 2 else 4 if s < G_GLU else 5 if s % 2 or s <= SB_FROM else 6
        plan.append([])
        while room and min(done) < CONV_K:
            ready = [c for c in range(CC) if done[c] < CONV_K and s >= 2 * c + 2]
            c = min(ready, key=lambda c: (done[c], c))
            if not ready or (len(ready) == 1 and done[c] == CONV_K):
                break
            plan[-1].append((c, done[c], n, last[c]))
            last[c], done[c], n, room = n, done[c] + 1, n + 1, room - 1
    assert n == CC * CONV_K
    return plan


TAPS = tap_plan()

FOX_FROM = 7
RET_S, RET_T, RET_V = 17, 19, 20

WARM_UP, COOL = 6, 9

FV, FQ, FK, RQ, RK, RV, RG = 0, 4, 5, 12, 14, 16, 20
ROTQ, ROTK, RET_O, RET_VAR = 0, 2, 12, 4
VV, QQ, GSB, GCV = 0, 4, 8, 16


def build(nc, hT, meta2, w8, w11, wff, fbias, prm_d, cst1_d, cst_d, outT):
    ctx = ExitStack()
    with ctx:
        def sb(name, shape, dt=F32):
            return ctx.enter_context(nc.sbuf_tensor(name, shape, dt))

        def sem(name):
            return ctx.enter_context(nc.semaphore(name))

        raw = sb("raw", [P, 4, S11])
        whi = sb("whi", [P, 4, S11], F32R)
        wlo = sb("wlo", [P, 4, S11], F32R)
        h = sb("h", [P, DC, T])
        xh = sb("xh", [P, DC, T], F32R)
        xl = sb("xl", [P, DC, T], F32R)
        ah = sb("ah", [P, FC, T], F32R)
        al = sb("al", [P, FC, T], F32R)
        proj = sb("proj", [P, 24, T])
        vT = sb("vT", [P, 3, 512])
        scr = sb("scr", [P, SC_N])
        prm = sb("prm", [P, PRM_N])
        cst = sb("cst", [P, 3 * P + SBW])
        m2 = sb("m2", [P, DC, META])
        acc = sb("acc", [P, T])
        sq = sb("sq", [P, 2, T])
        rinv = sb("rinv", [P, T])

        ones = cst[:, 0:P]
        ident = cst[:, P:2 * P]
        trige = cst[:, 2 * P:3 * P]
        unseen = cst[:, 3 * P:3 * P + SBW]

        def s1(name):
            a, n = SC1[name]
            return scr[:, a:a + n]

        def s2(name):
            a, n = SC2[name]
            return scr[:, a:a + n]

        later, fmask, dist, cos, sin = (s1(x) for x in ("later", "mask", "dist", "cos", "sin"))
        prob, decay = (s1(x).rearrange("p (b n) -> p b n", b=2) for x in ("prob", "decay"))
        probT = s1("probT")
        wff_s, wffg = (s1(x).rearrange("p (k n) -> p k n", k=DC) for x in ("wff", "wffg"))
        ff_s, fe_s, csum, fb_s = (s1(x)[0:FOX_H, :] for x in ("ff", "fe", "csum", "fbias"))
        lf_s = s1("lf")
        mx, nmx, rsum, rsinv = (s1(x).rearrange("p (b n) -> p b n", b=2) for x in ("mx", "nmx", "rsum", "rinv"))
        kpad = s2("kpad").rearrange("p (c n) -> p c n", c=CC)
        u = s2("u").rearrange("p (c n) -> p c n", c=CC)
        y = s2("y").rearrange("p (c n) -> p c n", c=CC)
        soft, keep, attn = s2("soft"), s2("keep"), s2("attn")
        gate = s2("gate").rearrange("p (b n) -> p b n", b=2)
        actv = s2("act").rearrange("p (b n) -> p b n", b=2)
        upv = s2("up")
        prod = s2("prod").rearrange("p (b n) -> p b n", b=2)

        W = [ctx.enter_context(nc.psum_tensor(f"W{i}", [P, 512], F32)) for i in range(4)]
        X = [ctx.enter_context(nc.psum_tensor(f"X{i}", [P, 512], F32)) for i in range(4)]

        raw_landed = [sem(f"raw_landed{j}") for j in range(4)]
        hi_ready = [sem(f"hi_ready{j}") for j in range(4)]
        lo_ready = [sem(f"lo_ready{j}") for j in range(4)]
        mm_done = sem("mm_done")
        evac_done = sem("evac_done")
        xh_ready, xl_ready = sem("xh_ready"), sem("xl_ready")
        sq_ready, acc_done = sem("sq_ready"), sem("acc_done")
        acc_zero = sem("acc_zero")
        stat_mm, var_ready, sqrt_ready, r_ready = (sem(x) for x in ("stat_mm", "var_ready", "sqrt_ready", "r_ready"))
        conv_ready, act_ready = sem("conv_ready"), sem("act_ready")
        prod_ready = sem("prod_ready")
        ah_ready, al_ready = sem("ah_ready"), sem("al_ready")
        cv_step = sem("cv_step")
        zero_set, warm_set = sem("zero_set"), sem("warm_set")
        h_landed = [sem(f"h_landed{i}") for i in range(DC // 2)]
        prm_landed, cst_landed, c1_landed, m2_landed, ff_landed = (
            sem(x) for x in ("prm_landed", "cst_landed", "c1_landed", "m2_landed", "ff_landed"))
        wffg_ready, ff_mm, ff_step, ff_abs, ff_log, lt_mm, lf_ready, c_mm, c_ready = (
            sem(x) for x in ("wffg_ready", "ff_mm", "ff_step", "ff_abs", "ff_log", "lt_mm", "lf_ready", "c_mm", "c_ready"))
        vt_mm, vt_ready = sem("vt_mm"), sem("vt_ready")
        fl_mm, fl_max, fl_exp, fp_step, fp_ready, ft_mm, ft_ready, fo_mm, fo_hi, fo_lo, fl_step = (
            sem(x) for x in ("fl_mm", "fl_max", "fl_exp", "fp_step", "fp_ready", "ft_mm", "ft_ready", "fo_mm",
                             "fo_hi", "fo_lo", "fl_step"))
        rot_step, rot_ready = sem("rot_step"), sem("rot_ready")
        rs_mm, rd_ready, rs_ready, ro_mm, ro_copy, ro_sq, rv_mm, rvar_ready, rsqrt_ready, rn_step, rg_ready, ro_ready, ro_hi, ro_lo = (
            sem(x) for x in ("rs_mm", "rd_ready", "rs_ready", "ro_mm", "ro_copy", "ro_sq", "rv_mm", "rvar_ready",
                             "rsqrt_ready", "rn_step", "rg_ready", "ro_ready", "ro_hi", "ro_lo"))
        trans_done = sem("trans_done")
        glu_sig, u_ready, conv_step = (sem(x) for x in ("glu_sig", "u_ready", "conv_step"))
        v2_mm, v2_ready = sem("v2_mm"), sem("v2_ready")
        z_mm, soft_step, sp_step, keep_ready, cum_mm, arg_ready, attn_ready, o_mm, o_hi, o_lo = (
            sem(x) for x in ("z_mm", "soft_step", "sp_step", "keep_ready", "cum_mm", "arg_ready",
                             "attn_ready", "o_mm", "o_hi", "o_lo"))
        ln_step, ln_sum, ln_mm, ln_cent, ln_sq, ln_var, ln_sqrt, ln_rcp, ln_norm, ln_silu, s_hi, s_lo = (
            sem(x) for x in ("ln_step", "ln_sum", "ln_mm", "ln_cent", "ln_sq", "ln_var", "ln_sqrt", "ln_rcp", "ln_norm",
                             "ln_silu", "s_hi", "s_lo"))
        sig_ready, mix_ready, mix_hi, mix_lo = (
            sem(x) for x in ("sig_ready", "mix_ready", "mix_hi", "mix_lo"))
        out_ready, out_sent = sem("out_ready"), sem("out_sent")

        block = ctx.enter_context(nc.Block())

        def split_base(p):
            return 8 * p if isinstance(p, int) and p <= 2 else 8 * p - 8

        POOL_ALL, SHARED = (0, 1, 2, 3), (0, 2)

        def ahead(j, own, nxt):
            return (0, 3, *own) if j == 0 else (1, j - 1, *nxt)

        K8A, K8S, K11 = (S8, POOL_ALL), (S8, SHARED), (S11, SHARED)

        @block.sync
        def _(sp):
            def load(g, src, j, cols, first=False):
                if not first:
                    sp.wait_ge(hi_ready[j], g)
                    sp.wait_ge(lo_ready[j], g)
                sp.dma_start(raw[:, j, 0:cols], src).then_inc(raw_landed[j], 16)

            def slab8(n):
                return w8[bass.ds(n, 1), :, :].rearrange("a p c -> p (a c)")

            def slab11(n):
                return w11[bass.ds(n, 1), :, :].rearrange("a p c -> p (a c)")

            def loads(n, g, slab, first_slab, cols):
                with sp.Fori(0, n) as i:
                    for j in range(4):
                        load(g + i, slab(first_slab + 4 * i + j), j, cols)

            load(0, slab8(0), 0, S8, first=True)
            sp.dma_start(prm[:, :], prm_d).then_inc(prm_landed, 16)
            for i in range(DC // 2):
                sp.dma_start(h[:, 2 * i:2 * i + 2, :], hT[:, 2 * i:2 * i + 2, :]).then_inc(h_landed[i], 16)
            load(0, slab8(1), 1, S8, first=True)
            sp.dma_start(wff_s, wff).then_inc(ff_landed, 16)
            sp.dma_start(fb_s, fbias).then_inc(ff_landed, 16)
            load(0, slab8(2), 2, S8, first=True)
            sp.dma_start(cst[:, :], cst_d).then_inc(cst_landed, 16)
            load(0, slab8(3), 3, S8, first=True)
            sp.dma_start(scr[:, 0:SC1_CONST], cst1_d).then_inc(c1_landed, 16)
            sp.dma_start(m2[:, :, :], meta2).then_inc(m2_landed, 16)
            loads(N_QKV1 - 1, 1, slab8, W8_QKV1 + 4, S8)
            loads(N_WO, G_WO1, slab8, W8_WO1, S8)
            loads(N_UP, G_UP1, slab8, W8_UP1, S8)
            loads(N_DN, G_DN1, slab11, 0, S11)
            with sp.Fori(0, LAYERS) as l:
                g, n8, n11 = G_LAYER + PER_LAYER * l, W8_LAYER + W8_PER * l, W11_LAYER + W11_PER * l
                loads(N_UP, g + L_UPA, slab8, n8 + W8_UPA, S8)
                loads(N_DN, g + L_DNA, slab11, n11, S11)
                loads(N_MIX, g + L_MIX, slab8, n8 + W8_MIX, S8)
                loads(N_AC, g + L_AC, slab8, n8 + W8_AC, S8)
                loads(N_WO, g + L_WO, slab8, n8 + W8_WO, S8)
                loads(N_UP, g + L_UPB, slab8, n8 + W8_UPB, S8)
                loads(N_DN, g + L_DNB, slab11, n11 + 16, S11)
            for j in range(3):
                load(G_LAYER + PER_LAYER * LAYERS, slab8(W8_TOTAL - 4 + j), j, S8)
            for m in range(0, DC, 2):
                sp.wait_ge(out_ready, m + 2)
                sp.dma_start(outT[:, m:m + 2, :], h[:, m:m + 2, META:T]).then_inc(out_sent, 16)
            sp.wait_ge(out_sent, 16 * DC // 2)

        @block.gpsimd
        def _(pool):
            def lo(g, j, cols):
                pool.wait_ge(hi_ready[j], g + 1)
                pool.tensor_tensor(wlo[:, j, 0:cols], raw[:, j, 0:cols], whi[:, j, 0:cols].bitcast(F32),
                                   ALU.subtract).then_inc(lo_ready[j], 1)

            def los(n, g, kind):
                cols, slots = kind
                with pool.Fori(0, n) as i:
                    for j in slots:
                        lo(g + i, j, cols)

            def first_los(g):
                for j in SHARED:
                    lo(g, j, S8)

            for j in range(2, 4):
                lo(0, j, S8)
            los(N_QKV1 - 1, 1, K8A)
            los(N_WO, G_WO1, K8A)
            los(N_UP, G_UP1, K8S)
            los(N_DN, G_DN1, K11)
            first_los(G_LAYER)
            pool.wait_ge(acc_zero, 4)
            for m in range(DC):
                pool.wait_ge(sq_ready, 8 * 3 + m + 1)
                if m:
                    pool.wait_ge(acc_done, 8 * 3 + m)
                pool.tensor_tensor(acc[:, :], acc[:, :], sq[:, m % 2, :], ALU.add).then_inc(acc_done, 1)
            with pool.Fori(0, LAYERS) as l:
                g = G_LAYER + PER_LAYER * l
                los(N_UP - 1, g + L_UPA + 1, K8S)
                los(N_DN, g + L_DNA, K11)
                los(N_MIX, g + L_MIX, K8A)
                los(N_AC, g + L_AC, K8A)
                los(N_WO, g + L_WO, K8S)
                los(N_UP, g + L_UPB, K8S)
                los(N_DN, g + L_DNB, K11)
                first_los(g + PER_LAYER)

        @block.scalar
        def _(act):
            def hi(g, j, cols, first=False):
                act.wait_ge(raw_landed[j], 16 * g + 16)
                if not first:
                    act.wait_ge(mm_done, 4 * g + j - 3)
                act.activation(whi[:, j, 0:cols], raw[:, j, 0:cols], ACT.Copy).then_inc(hi_ready[j], 1)

            def hi_ahead(g, j, own, nxt):
                dg, slot, cols, _ = ahead(j, own, nxt)
                hi(g + dg, slot, cols, first=isinstance(g, int) and g + dg == 0)

            def sqrt_stat(p, t=0):
                act.wait_ge(var_ready, p + 1)
                act.activation(rinv[:, t:], rinv[:, t:], ACT.Sqrt).then_inc(sqrt_ready, 1)

            def split_x(p, m, t=0):
                act.activation(xh[:, bass.ds(m, 1), t:], h[:, bass.ds(m, 1), t:], ACT.Copy,
                               scale=prm[:, bass.ds(PRM_G + 8 * p + m, 1)]).then_inc(xh_ready, 1)

            def square(p, m, b, t=0):
                act.activation(sq[:, b, t:], h[:, bass.ds(m, 1), t:], ACT.Square).then_inc(sq_ready, 1)

            def ffn_up(g, f, p, own, nxt, conv=False):
                ta, t = (T_A, T_B) if conv else (0, 0)

                def group(i, own, nxt, first=False):
                    for j in range(4):
                        b, c = j // 2, 2 * i + j // 2
                        if not first:
                            hi_ahead(g + i, j, own, nxt)
                        elif j == 2:
                            hi_ahead(g + i, 3, own, nxt)
                        if j % 2 == 0:
                            if conv:
                                act.wait_ge(conv_ready, c + 1)
                            else:
                                act.wait_ge(evac_done, 4 * (g + i) + j + 1)
                            act.activation(actv[:, b, t:], gate[:, b, 2 + t:T + 2], ACT.Silu).then_inc(act_ready, 1)
                        else:
                            act.wait_ge(prod_ready, FC * f + c + 1)
                            act.activation(ah[:, bass.ds(c, 1), t:], prod[:, b, t:], ACT.Copy).then_inc(ah_ready, 1)
                for j in range(2):
                    hi_ahead(g, j, own, own)
                sqrt_stat(p, ta)
                hi_ahead(g, 2, own, own)
                act.preload_act_table_set("silu_and_others")
                group(0, own, own, first=True)
                with act.Fori(1, N_UP - 1) as i:
                    group(i, own, own)
                group(N_UP - 1, own, nxt)

            def residual_tail(p, m, b, n, t):
                act.wait_ge(acc_done, 8 * p + m - 1)
                act.wait_ge(evac_done, n)
                square(p, m, b, t)
                if not (isinstance(p, int) and p == 2):
                    split_x(p, m, t)

            def ffn_down(g, p, nxt, t=0):
                def group(i, nxt):
                    for j in range(4):
                        hi_ahead(g + i, j, K11, nxt)
                        if j % 2:
                            residual_tail(p, 2 * i + j // 2, j // 2, 4 * (g + i) + j + 1, t)
                act.preload_act_table_set("sqrt_and_others")
                with act.Fori(0, N_DN - 1) as i:
                    group(i, K11)
                group(N_DN - 1, nxt)

            def out_proj(g, p, own=K8S, t=0, rounded=0):
                act.preload_act_table_set("sqrt_and_others")
                for i in range(N_WO):
                    for j in range(4):
                        if 4 * i + j >= rounded:
                            hi_ahead(g + i, j, own, own if i < N_WO - 1 else K8S)
                        residual_tail(p, 4 * i + j, j % 2, 4 * (g + i) + j + 1, t)

            hi(0, 0, S8, first=True)
            act.wait_ge(prm_landed, 16)
            for m in range(DC):
                act.wait_ge(h_landed[m // 2], 16)
                split_x(0, m)
            for j in (1, 2):
                hi(0, j, S8, first=True)
            for m in range(DC):
                if m >= 2:
                    act.wait_ge(acc_done, m - 1)
                square(0, m, m % 2)

            def fox_exp(hd):
                act.wait_ge(fl_max, hd + 1)
                for b in range(3):
                    r, at, w = FOX_BLK[b]
                    act.activation(prob[0:r, hd % 2, at:at + w], prob[0:r, hd % 2, at:at + w], ACT.Exp,
                                   bias=nmx[0:r, hd % 2, b:b + 1],
                                   accum_out=rsum[0:r, hd % 2, b:b + 1]).then_inc(fl_exp, 1)

            def fox_probT(hd):
                act.wait_ge(ft_mm, hd + 1)
                if hd >= 1:
                    act.wait_ge(fo_mm, hd)
                act.activation(probT[:, 0:416], X[2][:, 0:416], ACT.Copy).then_inc(ft_ready, 1)
                act.activation(probT[0:16, 416:SBW], X[2][0:16, 416:SBW], ACT.Copy).then_inc(ft_ready, 1)

            def fox_hi(c):
                act.wait_ge(fo_mm, 2 * c + 2)
                act.activation(ah[:, CC + c, :], X[3][:, 0:T], ACT.Copy).then_inc(fo_hi, 1)

            def ret_decay(hd):
                if hd >= 2:
                    act.wait_ge(ro_mm, hd - 1)
                elif hd == 1:
                    act.wait_ge(rot_ready, 4)
                else:
                    act.wait_ge(c1_landed, 16)
                act.activation(decay[:, hd % 2, :], dist, ACT.Exp,
                               scale=float(np.log1p(-2.0 ** (-5.0 - hd)))).then_inc(rd_ready, 1)

            def ret_square(hd):
                act.wait_ge(ro_mm, hd + 1)
                act.activation(proj[:, RET_O + hd, :], X[2][:, 0:T], ACT.Copy).then_inc(ro_copy, 1)
                if hd >= 2:
                    act.wait_ge(rv_mm, hd - 1)
                act.activation(sq[:, hd % 2, :], X[2][:, 0:T], ACT.Square).then_inc(ro_sq, 1)

            def ret_sqrt(hd):
                act.wait_ge(rvar_ready, hd + 1)
                act.activation(proj[:, RET_VAR + hd, :], proj[:, RET_VAR + hd, :], ACT.Sqrt).then_inc(rsqrt_ready, 1)

            for s in range(4 * N_QKV1):
                if 0 <= s - FOX_FROM - 3 < FOX_H:
                    fox_probT(s - FOX_FROM - 3)
                hi_ahead(s // 4, s % 4, K8A, K8A)
                if s == 2:
                    sqrt_stat(0)
                    act.preload_act_table_set("natural_log_exp_and_others")
                if s == 3:
                    act.wait_ge(ff_abs, 1)
                    act.activation(fe_s, fe_s, ACT.Exp, scale=-1.0).then_inc(ff_log, 1)
                    act.wait_ge(ff_log, 1)
                    act.activation(fe_s, fe_s, ACT.Ln, bias=1.0).then_inc(ff_log, 1)
                if 0 <= s - FOX_FROM - 1 < FOX_H:
                    fox_exp(s - FOX_FROM - 1)
                c, late = divmod(s - FOX_FROM - 5, 2)
                if not late and 0 <= c < CC:
                    fox_hi(c)
                if RET_S - 1 <= s <= RET_S:
                    ret_decay(s - RET_S + 1)
                if s > RET_V:
                    ret_square(s - RET_V - 1)
                if RET_V < s <= RET_V + 2:
                    ret_decay(s - RET_V + 1)
                if s == RET_V + 2:
                    act.preload_act_table_set("sqrt_and_others")
                if s >= RET_V + 2:
                    ret_sqrt(s - RET_V - 2)
            hi_ahead(G_WO1, 0, K8A, K8A)
            ret_square(3)
            for hd in range(2, RET_H):
                ret_sqrt(hd)
            act.wait_ge(evac_done, 4 * N_QKV1)
            act.activation(proj[:, RG:RG + 4, :], proj[:, RG:RG + 4, :], ACT.Silu).then_inc(rg_ready, 1)
            for hd in range(RET_H):
                act.wait_ge(ro_ready, hd + 1)
                act.activation(ah[:, hd, :], proj[:, RET_O + hd, :], ACT.Copy).then_inc(ro_hi, 1)
            for j in (1, 2, 3):
                hi_ahead(G_WO1, j, K8A, K8A)
            out_proj(G_WO1, 1, K8A, T_A, rounded=4)
            ffn_up(G_UP1, 0, 1, K8S, K11, conv=True)
            ffn_down(G_DN1, 2, K8S, T_B)
            sqrt_stat(2, T_B)
            for m in range(DC):
                act.wait_ge(trans_done, m + 2)
                split_x(3, m)
                act.wait_ge(acc_done, 8 * 3 + m - 1)
                square(3, m, m % 2)

            def mixer(g, l, p):
                def soften(hd):
                    n = 3 * (SB_H * l + hd)
                    act.wait_ge(z_mm, SB_H * l + hd + 1)
                    if hd:
                        act.wait_ge(keep_ready, SB_H * l + hd)
                    act.activation(soft, X[hd % 2][:, 0:SBW], ACT.Abs).then_inc(soft_step, 1)
                    act.wait_ge(soft_step, n + 1)
                    act.activation(soft, soft, ACT.Exp, scale=-1.0).then_inc(soft_step, 1)
                    act.wait_ge(soft_step, n + 2)
                    act.activation(soft, soft, ACT.Ln, bias=1.0).then_inc(soft_step, 1)

                def weights(hd):
                    act.wait_ge(arg_ready, SB_H * l + hd + 1)
                    act.activation(attn, attn, ACT.Exp).then_inc(attn_ready, 1)

                def out_hi(c):
                    act.wait_ge(o_mm, SB_H * l + 2 * c + 2)
                    act.activation(ah[:, c, :], X[2][:, 0:T], ACT.Copy).then_inc(o_hi, 1)

                for s in range(4 * N_MIX):
                    hd, late = divmod(s - SB_FROM - 1, 2)
                    if not late and 0 <= hd < SB_H:
                        soften(hd)
                    if not late and 1 <= hd <= SB_H:
                        weights(hd - 1)
                    if not late and hd >= 3 and hd % 2:
                        out_hi((hd - 3) // 2)
                    if s == LN_FROM + 3:
                        for c in range(CC):
                            act.wait_ge(ln_cent, CC * l + c + 1)
                            act.activation(u[:, c, CONV_K - 1:], y[:, c, :], ACT.Square).then_inc(ln_sq, 1)
                    if s == LN_FROM + 6:
                        act.wait_ge(ln_var, l + 1)
                        act.activation(acc[:, :], acc[:, :], ACT.Sqrt).then_inc(ln_sqrt, 1)
                        act.preload_act_table_set("silu_and_others")
                    if s == LN_FROM + 8:
                        for c in range(CC):
                            act.wait_ge(ln_norm, CC * l + c + 1)
                            act.activation(y[:, c, :], y[:, c, :], ACT.Silu, scale=prm[:, bass.ds(PRM_LNG + CC * l + c, 1)],
                                           bias=prm[:, bass.ds(PRM_LNB + CC * l + c, 1)]).then_inc(ln_silu, 1)
                        act.preload_act_table_set("sigmoid_and_others")
                    hi_ahead(g + s // 4, s % 4, K8A, K8A)
                    if s == 1:
                        sqrt_stat(p - 1)
                    if s < G_GLU and s % 2:
                        c = s // 2
                        act.wait_ge(evac_done, 4 * g + s + 1)
                        act.activation(proj[:, 4 + c, :], proj[:, 4 + c, :], ACT.Sigmoid).then_inc(glu_sig, 1)
                    if s == G_GLU:
                        act.preload_act_table_set("natural_log_exp_and_others")
                ga = g + N_MIX
                act.wait_ge(evac_done, 4 * ga - DC)
                act.activation(proj[:, GSB:GSB + DC, :], proj[:, GSB:GSB + DC, :], ACT.Sigmoid).then_inc(sig_ready, 1)
                hi_ahead(ga, 0, K8A, K8A)
                for c in range(CC):
                    act.wait_ge(ln_silu, CC * l + c + 1)
                    act.activation(ah[:, CC + c, :], y[:, c, :], ACT.Copy).then_inc(s_hi, 1)
                hi_ahead(ga, 1, K8A, K8A)
                act.wait_ge(evac_done, 4 * ga)
                act.activation(proj[:, GCV:GCV + DC, :], proj[:, GCV:GCV + DC, :], ACT.Sigmoid).then_inc(sig_ready, 1)
                hi_ahead(ga, 2, K8A, K8A)
                hi_ahead(ga, 3, K8A, K8A)
                for j in range(4):
                    hi_ahead(ga + 1, j, K8A, K8S)
                    for m in (2 * j, 2 * j + 1):
                        act.wait_ge(mix_ready, DC * l + m + 1)
                        act.activation(ah[:, DC + m, :], proj[:, GSB + m, :], ACT.Copy).then_inc(mix_hi, 1)
                out_proj(ga + N_AC, p)

            with act.Fori(0, LAYERS) as l:
                g, p = G_LAYER + PER_LAYER * l, 4 + 3 * l
                ffn_up(g + L_UPA, 1 + 2 * l, p - 1, K8S, K11)
                ffn_down(g + L_DNA, p, K8A)
                mixer(g + L_MIX, l, p + 1)
                ffn_up(g + L_UPB, 2 + 2 * l, p + 1, K8S, K11)
                ffn_down(g + L_DNB, p + 2, K8S)
            sqrt_stat(3 + 3 * LAYERS)

        @block.vector
        def _(dve):
            def lo_ahead(g, j, own, nxt):
                dg, slot, cols, pools = ahead(j, own, nxt)
                if slot not in pools:
                    dve.wait_ge(hi_ready[slot], g + dg + 1)
                    dve.tensor_tensor(wlo[:, slot, 0:cols], raw[:, slot, 0:cols], whi[:, slot, 0:cols].bitcast(F32),
                                      ALU.subtract).then_inc(lo_ready[slot], 1)

            def norm_factor(p, t=0):
                dve.wait_ge(stat_mm, p + 1)
                dve.tensor_scalar(rinv[:, t:], X[3][:, t:T], 1.0 / D, EPS, ALU.mult, ALU.add).then_inc(var_ready, 1)
                dve.wait_ge(sqrt_ready, p + 1)
                dve.reciprocal(rinv[:, t:], rinv[:, t:]).then_inc(r_ready, 1)

            def scaled(out, bank, n, t=0):
                dve.wait_ge(mm_done, n)
                return dve.tensor_tensor(out, W[bank][:, t:T], rinv[:, t:], ALU.mult)

            def take_lo(p, m, t=0):
                dve.wait_ge(xh_ready, split_base(p) + m + 1)
                dve.scalar_tensor_tensor(xl[:, bass.ds(m, 1), t:], h[:, bass.ds(m, 1), t:],
                                         prm[:, bass.ds(PRM_G + 8 * p + m, 1)],
                                         xh[:, bass.ds(m, 1), t:].bitcast(F32), ALU.mult, ALU.subtract).then_inc(xl_ready, 1)

            def add_square(p, m, b, t=0, first=False):
                dve.wait_ge(sq_ready, 8 * p + m + 1)
                dve.wait_ge(acc_zero, p + 1)
                if not first:
                    dve.wait_ge(acc_done, 8 * p + m)
                dve.tensor_tensor(acc[:, t:], acc[:, t:], sq[:, b, t:], ALU.add).then_inc(acc_done, 1)

            def residual(p, m, b, bank, n, slabs, coef, t):
                dve.wait_ge(mm_done, n)
                dve.scalar_tensor_tensor(h[:, bass.ds(m, 1), t:], W[bank][:, t:T], coef, h[:, bass.ds(m, 1), t:],
                                         ALU.mult, ALU.add).then_inc(evac_done, slabs)
                dve.wait_ge(evac_done, n)
                add_square(p, m, b, t)
                if not (isinstance(p, int) and p == 2):
                    take_lo(p, m, t)

            def clear_sum():
                dve.memset(acc[:, :], 0.0).then_inc(acc_zero, 1)

            def ffn_up(g, f, p, own, nxt, conv=False):
                ta, tb = (T_A, T_B) if conv else (0, 0)
                def group(i, own, nxt, first=False):
                    for j in range(4):
                        b, c = j // 2, 2 * i + j // 2
                        n = 4 * (g + i) + j + 1
                        if first and j == 0:
                            dve.wait_ge(r_ready, p + 1)
                        if j % 2 == 0:
                            scaled(gate[:, b, 2 + ta:T + 2], j, n, ta).then_inc(evac_done, 1)
                        if j % 2 == 0 and conv:
                            dve.wait_ge(evac_done, n)
                            w = [prm[:, bass.ds(PRM_CW1 + CONV_W * c + k, 1)] for k in range(CONV_W)]
                            dve.tensor_scalar(actv[:, b, tb:], gate[:, b, tb:T], w[0], prm[:, bass.ds(PRM_CB1 + c, 1)],
                                              ALU.mult, ALU.add).then_inc(cv_step, 1)
                            dve.wait_ge(cv_step, 2 * c + 1)
                            dve.scalar_tensor_tensor(actv[:, b, tb:], gate[:, b, tb + 1:T + 1], w[1], actv[:, b, tb:],
                                                     ALU.mult, ALU.add).then_inc(cv_step, 1)
                            dve.wait_ge(cv_step, 2 * c + 2)
                            dve.scalar_tensor_tensor(gate[:, b, tb + 2:T + 2], gate[:, b, tb + 2:T + 2], w[2],
                                                     actv[:, b, tb:], ALU.mult, ALU.add).then_inc(conv_ready, 1)
                        if j % 2:
                            scaled(upv[:, tb:], j, n, tb).then_inc(evac_done, 1)
                            dve.wait_ge(evac_done, n)
                            dve.wait_ge(act_ready, FC * f + c + 1)
                            dve.tensor_tensor(prod[:, b, tb:], actv[:, b, tb:], upv[:, tb:], ALU.mult).then_inc(prod_ready, 1)
                        if not (first and j in (0, 2)):
                            lo_ahead(g + i, j, own, nxt)
                        if j >= 2:
                            cc = 2 * i + j - 2
                            dve.wait_ge(ah_ready, FC * f + cc + 1)
                            dve.tensor_tensor(al[:, bass.ds(cc, 1), tb:], prod[:, j - 2, tb:],
                                              ah[:, bass.ds(cc, 1), tb:].bitcast(F32), ALU.subtract).then_inc(al_ready, 1)
                lo_ahead(g, 0, own, own)
                norm_factor(p, ta)
                lo_ahead(g, 2, own, own)
                group(0, own, own, first=True)
                with dve.Fori(1, N_UP - 1) as i:
                    group(i, own, own)
                group(N_UP - 1, own, nxt)

            def ffn_down(g, p, nxt, coef, t=0):
                def group(i, nxt):
                    for j in range(4):
                        lo_ahead(g + i, j, K11, nxt)
                        if j % 2:
                            residual(p, 2 * i + j // 2, j // 2, j - 1, 4 * (g + i) + j + 1, 2, coef, t)
                clear_sum()
                with dve.Fori(0, N_DN - 1) as i:
                    group(i, K11)
                group(N_DN - 1, nxt)

            def out_proj(g, p, own=K8S, t=0):
                clear_sum()
                for i in range(N_WO):
                    for j in range(4):
                        lo_ahead(g + i, j, own, own if i < N_WO - 1 else K8S)
                        residual(p, 4 * i + j, j % 2, j, 4 * (g + i) + j + 1, 1, 1.0, t)

            dve.memset(vT[:, 0, :], 0.0).then_inc(warm_set, 1)
            clear_sum()
            dve.memset(s1("mx"), 0.0).then_inc(zero_set, 1)
            dve.memset(s1("rsum"), 1.0).then_inc(zero_set, 1)

            def first_lo(j):
                dve.wait_ge(hi_ready[j], 1)
                dve.tensor_tensor(wlo[:, j, 0:S8], raw[:, j, 0:S8], whi[:, j, 0:S8].bitcast(F32),
                                  ALU.subtract).then_inc(lo_ready[j], 1)

            first_lo(0)
            dve.wait_ge(prm_landed, 16)
            for m in range(DC):
                dve.wait_ge(h_landed[m // 2], 16)
                take_lo(0, m)
            first_lo(1)
            dve.wait_ge(ff_landed, 32)
            for k in range(DC):
                dve.tensor_scalar(wffg[:, k, :], wff_s[:, k, :], prm[:, PRM_G + k:PRM_G + k + 1], None,
                                  ALU.mult).then_inc(wffg_ready, 1)
            for m in range(DC):
                add_square(0, m, m % 2, first=m == 0)

            def rows(b):
                return BLK[b][1] - BLK[b][0]

            def forget_gates():
                dve.wait_ge(ff_mm, 1)
                dve.tensor_tensor(ff_s, X[2][0:FOX_H, 0:T], rinv[0:FOX_H, :], ALU.mult).then_inc(ff_step, 1)
                dve.wait_ge(ff_step, 1)
                dve.tensor_scalar(ff_s, ff_s, fb_s, None, ALU.add).then_inc(ff_step, 1)
                dve.wait_ge(ff_step, 2)
                dve.scalar_tensor_tensor(fe_s, ff_s, -1.0, ff_s, ALU.mult, ALU.max).then_inc(ff_abs, 1)

            def forget_logs():
                dve.wait_ge(ff_log, 2)
                dve.scalar_tensor_tensor(ff_s, ff_s, 0.0, fe_s, ALU.min, ALU.subtract).then_inc(ff_step, 1)

            def forget_tokens():
                dve.wait_ge(lt_mm, 1)
                for b in range(3):
                    dve.tensor_scalar(lf_s[0:rows(b), FOX_H * b:FOX_H * b + FOX_H], X[2][0:rows(b), FOX_H * b:FOX_H * b + FOX_H],
                                      -1.0 / FOX_DH ** -0.5, None, ALU.mult).then_inc(lf_ready, 1)

            def fox_max(hd):
                dve.wait_ge(fl_mm, hd + 1)
                if hd == 0:
                    dve.wait_ge(zero_set, 2)
                if hd >= 2:
                    dve.wait_ge(ft_mm, hd - 1)
                for b in range(3):
                    r, at, w = FOX_BLK[b]
                    src = X[0][0:r, at:at + w] if b < 2 else X[1][0:r, 0:T]
                    dve.tensor_tensor_reduce(prob[0:r, hd % 2, at:at + w], src, fmask[0:r, at:at + w], FOX_DH ** -0.5, -3.0e38,
                                             ALU.add, ALU.max, mx[0:r, hd % 2, b:b + 1]).then_inc(fl_step, 1)
                dve.wait_ge(fl_step, 3 * hd + 3)
                dve.tensor_scalar(nmx[:, hd % 2, 0:3], mx[:, hd % 2, 0:3], -1.0, None, ALU.mult).then_inc(fl_max, 1)

            def fox_probs(hd):
                dve.wait_ge(fl_exp, 3 * hd + 3)
                dve.reciprocal(rsinv[:, hd % 2, 0:3], rsum[:, hd % 2, 0:3]).then_inc(fp_step, 1)
                dve.wait_ge(fp_step, hd + 1)
                for b in range(3):
                    r, at, w = FOX_BLK[b]
                    dve.tensor_scalar(prob[0:r, hd % 2, at:at + w], prob[0:r, hd % 2, at:at + w],
                                      rsinv[0:r, hd % 2, b:b + 1], None, ALU.mult).then_inc(fp_ready, 1)

            def fox_lo(c):
                dve.wait_ge(fo_hi, c + 1)
                dve.tensor_tensor(al[:, CC + c, :], X[3][:, 0:T], ah[:, CC + c, :].bitcast(F32),
                                  ALU.subtract).then_inc(fo_lo, 1)

            def values_on_tokens(k, b, bank):
                dve.wait_ge(vt_mm, k + 1)
                dve.tensor_copy(vT[0:rows(b), b, :], X[bank][0:rows(b), :]).then_inc(vt_ready, 1)

            def rotary(k, src, dst):
                x1, x2 = proj[:, src, :], proj[:, src + 1, :]
                t1, t2 = decay[:, 1, 0:T], sq[:, 0, :]
                n = 4 * k
                for a, b, op, out in ((cos, sin, ALU.subtract, dst), (sin, cos, ALU.add, dst + 1)):
                    if n:
                        dve.wait_ge(rot_ready, n // 2)
                    dve.tensor_tensor(t1, x1, a, ALU.mult).then_inc(rot_step, 1)
                    dve.tensor_tensor(t2, x2, b, ALU.mult).then_inc(rot_step, 1)
                    n += 2
                    dve.wait_ge(rot_step, n)
                    dve.tensor_tensor(proj[:, out, :], t1, t2, op).then_inc(rot_ready, 1)

            def ret_weights(hd):
                dve.wait_ge(rs_mm, hd + 1)
                dve.wait_ge(rd_ready, hd + 1)
                for b in range(3):
                    r, w, at = rows(b), T - RET_FROM[b], RET_AT[b]
                    src = X[0][0:r, 0:w] if b == 0 else X[1][0:r, at - RET_AT[1]:at - RET_AT[1] + w]
                    dve.scalar_tensor_tensor(decay[0:r, hd % 2, at:at + w], src, RET_DK ** -0.5,
                                             decay[0:r, hd % 2, at:at + w], ALU.mult, ALU.mult).then_inc(rs_ready, 1)

            def ret_var(hd):
                dve.wait_ge(rv_mm, hd + 1)
                dve.tensor_scalar(proj[:, RET_VAR + hd, :], X[3][:, 0:T], 1.0 / RET_DV, EPS, ALU.mult,
                                  ALU.add).then_inc(rvar_ready, 1)

            def ret_norm(hd):
                dve.wait_ge(rsqrt_ready, hd + 1)
                dve.reciprocal(proj[:, RET_VAR + hd, :], proj[:, RET_VAR + hd, :]).then_inc(rn_step, 1)
                dve.wait_ge(rn_step, 2 * hd + 1)
                dve.scalar_tensor_tensor(proj[:, RET_O + hd, :], proj[:, RET_O + hd, :], prm[:, PRM_RETG + hd:PRM_RETG + hd + 1],
                                         proj[:, RET_VAR + hd, :], ALU.mult, ALU.mult).then_inc(rn_step, 1)

            for s in range(4 * N_QKV1):
                if s == 0:
                    norm_factor(0)
                    dve.wait_ge(r_ready, 1)
                if s == 5:
                    forget_tokens()
                if s == FOX_FROM:
                    dve.wait_ge(c_mm, 1)
                    dve.tensor_copy(csum, X[2][0:FOX_H, 0:T]).then_inc(c_ready, 1)
                if 0 <= s - FOX_FROM - 2 < FOX_H:
                    fox_probs(s - FOX_FROM - 2)
                if 0 <= s - FOX_FROM - 1 < FOX_H:
                    fox_max(s - FOX_FROM - 1)
                if RET_S < s <= RET_S + 2:
                    ret_weights(s - RET_S - 1)
                if RET_V < s <= RET_V + 2:
                    ret_weights(s - RET_V + 1)
                if s >= RET_V + 2:
                    ret_var(s - RET_V - 2)
                    ret_norm(s - RET_V - 2)
                scaled(proj[:, s, :], s % 4, s + 1).then_inc(evac_done, 1)
                if s == 2:
                    forget_gates()
                if s == 3:
                    forget_logs()
                if s == 6:
                    for b, bank in enumerate((0, 1, 3)):
                        values_on_tokens(b, b, bank)
                c, late = divmod(s - FOX_FROM - 5, 2)
                if not late and 0 <= c < CC:
                    fox_lo(c)
                if s == RQ + 2:
                    dve.wait_ge(evac_done, RQ + 2)
                    rotary(0, RQ, ROTQ)
                if s == RK + 2:
                    dve.wait_ge(evac_done, RK + 2)
                    rotary(1, RK, ROTK)
                if s == RET_T:
                    dve.wait_ge(fo_mm, FOX_H)
                    for b, bank in enumerate((2, 3, 0)):
                        values_on_tokens(3 + b, b, bank)
            ret_var(2)
            ret_var(3)
            ret_norm(2)
            ret_norm(3)
            dve.wait_ge(rg_ready, 1)
            for hd in range(RET_H):
                dve.wait_ge(rn_step, 2 * hd + 2)
                dve.tensor_tensor(proj[:, RET_O + hd, :], proj[:, RET_O + hd, :], proj[:, RG + hd, :],
                                  ALU.mult).then_inc(ro_ready, 1)
            for hd in range(RET_H):
                dve.wait_ge(ro_hi, hd + 1)
                dve.tensor_tensor(al[:, hd, :], proj[:, RET_O + hd, :], ah[:, hd, :].bitcast(F32),
                                  ALU.subtract).then_inc(ro_lo, 1)
            out_proj(G_WO1, 1, K8A, T_A)
            ffn_up(G_UP1, 0, 1, K8S, K11, conv=True)
            ffn_down(G_DN1, 2, K8S, 1.0, T_B)

            dve.wait_ge(m2_landed, 16)
            dve.tensor_copy(h[:, :, 0:META], m2[:, :, :]).then_inc(trans_done, 1)
            norm_factor(2, T_B)
            clear_sum()
            dve.wait_ge(r_ready, 3)
            for m in range(DC + 1):
                if m < DC:
                    dve.scalar_tensor_tensor(h[:, m, META:], h[:, m, META:], prm[:, PRM_G + 16 + m:PRM_G + 17 + m],
                                             rinv[:, META:], ALU.mult, ALU.mult).then_inc(trans_done, 1)
                if m:
                    dve.wait_ge(trans_done, m + 1)
                    take_lo(3, m - 1)
            dve.memset(kpad[:, :, T:], 0.0).then_inc(zero_set, 1)
            dve.memset(u[:, :, 0:CONV_K - 1], 0.0).then_inc(zero_set, 1)
            dve.wait_ge(zero_set, 4)

            def mixer(g, l, p):
                def taps(s):
                    for c, k, own, before in TAPS[s]:
                        w = prm[:, bass.ds(PRM_CW2 + CC * CONV_K * l + CONV_K * c + k, 1)]
                        if k == 0:
                            dve.wait_ge(u_ready, CC * l + c + 1)
                            dve.tensor_scalar(y[:, c, :], u[:, c, 0:T], w, prm[:, bass.ds(PRM_CB2 + CC * l + c, 1)],
                                              ALU.mult, ALU.add).then_inc(conv_step, 1)
                        else:
                            dve.wait_ge(conv_step, CC * CONV_K * l + before + 1)
                            dve.scalar_tensor_tensor(y[:, c, :], u[:, c, k:k + T], w, y[:, c, :], ALU.mult,
                                                     ALU.add).then_inc(conv_step, 1)

                def keeps(hd):
                    n = SB_H * l + hd
                    dve.wait_ge(soft_step, 3 * n + 3)
                    if hd:
                        dve.wait_ge(cum_mm, n)
                    dve.scalar_tensor_tensor(keep, X[hd % 2][:, 0:SBW], 0.0, soft, ALU.max, ALU.add).then_inc(sp_step, 1)
                    dve.wait_ge(sp_step, n + 1)
                    dve.scalar_tensor_tensor(keep, unseen, 1.0, keep, ALU.subtract, ALU.mult).then_inc(keep_ready, 1)

                def arguments(hd):
                    n = SB_H * l + hd
                    dve.wait_ge(cum_mm, n + 1)
                    if hd:
                        dve.wait_ge(o_mm, n)
                    dve.scalar_tensor_tensor(attn, unseen, NEG, X[hd % 2][:, 0:SBW], ALU.mult, ALU.add).then_inc(arg_ready, 1)

                def out_lo(c):
                    dve.wait_ge(o_hi, CC * l + c + 1)
                    dve.tensor_tensor(al[:, c, :], X[2][:, 0:T], ah[:, c, :].bitcast(F32), ALU.subtract).then_inc(o_lo, 1)

                ga = g + N_MIX
                for s in range(4 * N_MIX):
                    j, n = s % 4, 4 * g + s + 1
                    hd, late = divmod(s - SB_FROM - 1, 2)
                    if not late and 1 <= hd < SB_H + 1:
                        arguments(hd - 1)
                    if not late and 0 <= hd < SB_H:
                        keeps(hd)
                    if s == LN_FROM:
                        dve.wait_ge(conv_step, CC * CONV_K * (l + 1))
                        dve.tensor_tensor(acc[:, :], y[:, 0, :], y[:, 1, :], ALU.add).then_inc(ln_step, 1)
                        dve.tensor_tensor(sq[:, 0, :], y[:, 2, :], y[:, 3, :], ALU.add).then_inc(ln_step, 1)
                        dve.wait_ge(ln_step, 5 * l + 2)
                        dve.tensor_tensor(acc[:, :], acc[:, :], sq[:, 0, :], ALU.add).then_inc(ln_sum, 1)
                    if s == LN_FROM + 2:
                        dve.wait_ge(ln_mm, 2 * l + 1)
                        dve.tensor_scalar(sq[:, 1, :], X[3][:, 0:T], 1.0 / (CC * P), None, ALU.mult).then_inc(ln_step, 1)
                        dve.wait_ge(ln_step, 5 * l + 3)
                        for c in range(CC):
                            dve.tensor_tensor(y[:, c, :], y[:, c, :], sq[:, 1, :], ALU.subtract).then_inc(ln_cent, 1)
                    if s == LN_FROM + 4:
                        dve.wait_ge(ln_sq, CC * (l + 1))
                        dve.tensor_tensor(acc[:, :], u[:, 0, CONV_K - 1:], u[:, 1, CONV_K - 1:], ALU.add).then_inc(ln_step, 1)
                        dve.tensor_tensor(sq[:, 0, :], u[:, 2, CONV_K - 1:], u[:, 3, CONV_K - 1:], ALU.add).then_inc(ln_step, 1)
                        dve.wait_ge(ln_step, 5 * l + 5)
                        dve.tensor_tensor(acc[:, :], acc[:, :], sq[:, 0, :], ALU.add).then_inc(ln_sum, 1)
                    if s == LN_FROM + 6:
                        dve.wait_ge(ln_mm, 2 * l + 2)
                        dve.tensor_scalar(acc[:, :], X[3][:, 0:T], 1.0 / (CC * P), LN_EPS, ALU.mult, ALU.add).then_inc(ln_var, 1)
                    if s == LN_FROM + 7:
                        dve.wait_ge(ln_sqrt, l + 1)
                        dve.reciprocal(sq[:, 0, :], acc[:, :]).then_inc(ln_rcp, 1)
                        dve.wait_ge(ln_rcp, l + 1)
                        for c in range(CC):
                            dve.tensor_tensor(y[:, c, :], y[:, c, :], sq[:, 0, :], ALU.mult).then_inc(ln_norm, 1)
                    if s < G_GLU:
                        c = s // 2
                        scaled(proj[:, 4 + c if s % 2 else c, :], j, n).then_inc(evac_done, 1)
                        if s % 2:
                            dve.wait_ge(glu_sig, CC * l + c + 1)
                            dve.tensor_tensor(u[:, c, CONV_K - 1:], proj[:, c, :], proj[:, 4 + c, :],
                                              ALU.mult).then_inc(u_ready, 1)
                    elif s < G_V:
                        scaled(proj[:, VV + j, :], j, n).then_inc(evac_done, 1)
                    elif s < G_QK and s % 2 == 0:
                        dve.wait_ge(mm_done, n)
                        dve.scalar_tensor_tensor(proj[:, QQ + (s - G_V) // 2, :], W[j][:, 0:T], SB_DH ** -0.5, rinv[:, :],
                                                 ALU.mult, ALU.mult).then_inc(evac_done, 1)
                    elif s < G_QK:
                        scaled(kpad[:, (s - G_V) // 2, 0:T], j, n).then_inc(evac_done, 1)
                    else:
                        scaled(proj[:, GSB + s - G_QK, :], j, n).then_inc(evac_done, 1)
                    if G_V + 2 < s <= G_V + 5:
                        b = s - G_V - 3
                        dve.wait_ge(v2_mm, 3 * l + b + 1)
                        dve.tensor_copy(vT[0:rows(b), b, :], X[1 + b][0:rows(b), :]).then_inc(v2_ready, 1)
                    taps(s)
                    if not late and hd >= 3 and hd % 2:
                        out_lo((hd - 3) // 2)
                def attn_gate(j):
                    for m in (2 * j, 2 * j + 1):
                        dve.wait_ge(mm_done, 4 * ga + j + 1)
                        dve.wait_ge(sig_ready, 2 * l + 1)
                        ins = dve.tensor_tensor(proj[:, GSB + m, :], W[m % 4][:, 0:T], proj[:, GSB + m, :], ALU.mult)
                    ins.then_inc(evac_done, 1)

                for j in range(4):
                    attn_gate(j)
                    if j == 1:
                        for c in range(CC):
                            dve.wait_ge(s_hi, CC * l + c + 1)
                            dve.tensor_tensor(al[:, CC + c, :], y[:, c, :], ah[:, CC + c, :].bitcast(F32),
                                              ALU.subtract).then_inc(s_lo, 1)
                gb = ga + 1
                for j in range(4):
                    lo_ahead(gb, j, K8A, K8S)
                    for m in (2 * j, 2 * j + 1):
                        dve.wait_ge(mm_done, 4 * gb + j + 1)
                        dve.wait_ge(sig_ready, 2 * l + 2)
                        ins = dve.tensor_tensor(proj[:, GCV + m, :], W[m % 4][:, 0:T], proj[:, GCV + m, :], ALU.mult)
                    ins.then_inc(evac_done, 1)
                    dve.wait_ge(evac_done, 4 * gb + j + 1)
                    for m in (2 * j, 2 * j + 1):
                        dve.tensor_tensor(proj[:, GSB + m, :], proj[:, GSB + m, :], proj[:, GCV + m, :],
                                          ALU.add).then_inc(mix_ready, 1)
                    for m in (2 * j, 2 * j + 1):
                        dve.wait_ge(mix_hi, DC * l + m + 1)
                        dve.tensor_tensor(al[:, DC + m, :], proj[:, GSB + m, :], ah[:, DC + m, :].bitcast(F32),
                                          ALU.subtract).then_inc(mix_lo, 1)
                out_proj(ga + N_AC, p)

            with dve.Fori(0, LAYERS) as l:
                g, p = G_LAYER + PER_LAYER * l, 4 + 3 * l
                ffn_up(g + L_UPA, 1 + 2 * l, p - 1, K8S, K11)
                ffn_down(g + L_DNA, p, K8A, 0.5)
                norm_factor(p)
                dve.wait_ge(r_ready, p + 1)
                mixer(g + L_MIX, l, p + 1)
                ffn_up(g + L_UPB, 2 + 2 * l, p + 1, K8S, K11)
                ffn_down(g + L_DNB, p + 2, K8S, 0.5)
            norm_factor(3 + 3 * LAYERS)
            dve.wait_ge(r_ready, 4 + 3 * LAYERS)
            for m in range(DC):
                dve.scalar_tensor_tensor(h[:, m, META:T], h[:, m, META:T], prm[:, PRM_G + 72 + m:PRM_G + 73 + m],
                                         rinv[:, META:T], ALU.mult, ALU.mult).then_inc(out_ready, 1)

        @block.tensor
        def _(pe):
            def emptied(n):
                if not (isinstance(n, int) and n <= 0):
                    pe.wait_ge(evac_done, n)

            def slab(g, j, rhs, out, at=0, start=True, stop=True, each=None):
                pe.wait_ge(lo_ready[j], g + 1)
                for k, (mh, ml) in enumerate(rhs):
                    if each is not None and k >= each[2]:
                        pe.wait_ge(each[0], each[1] + k - each[2] + 1)
                    w = slice((at + k) * P, (at + k + 1) * P)
                    pe.matmul(out, whi[:, j, w], mh, start=start and k == 0, stop=False, skip_group_check=True)
                    pe.matmul(out, whi[:, j, w], ml, start=False, stop=False, skip_group_check=True)
                    ins = pe.matmul(out, wlo[:, j, w], mh, start=False, stop=stop and k == len(rhs) - 1,
                                    skip_group_check=True)
                return ins

            def x_rhs(t=0):
                return [(xh[:, k, t:], xl[:, k, t:]) for k in range(DC)]

            def a_rhs(t=0):
                return [(ah[:, k, t:], al[:, k, t:]) for k in range(FC)]

            X_RHS, A_RHS = x_rhs(), a_rhs()

            def stat(p, t=0):
                pe.wait_ge(acc_done, 8 * p + 8)
                pe.matmul(X[3][:, t:T], ones, acc[:, t:], start=True, stop=True, skip_group_check=True).then_inc(stat_mm, 1)

            def project(g, j, rhs, each=None, behind=3, t=0):
                emptied(4 * g + j - behind)
                slab(g, j, rhs, W[j][:, t:T], each=each).then_inc(mm_done, 1)

            def first_pair(g, rhss, each, behind=(3, 3), t=(0, 0)):
                for j in range(2):
                    emptied(4 * g + j - behind[j])
                    pe.wait_ge(lo_ready[j], g + 1)
                for k in range(DC):
                    pe.wait_ge(each[0], each[1] + k + 1)
                    w = slice(k * P, k * P + P)
                    for j in range(2):
                        mh, ml = rhss[j][k]
                        out = W[j][:, t[j]:T]
                        pe.matmul(out, whi[:, j, w], mh, start=k == 0, stop=False, skip_group_check=True)
                        pe.matmul(out, whi[:, j, w], ml, start=False, stop=False, skip_group_check=True)
                        ins = pe.matmul(out, wlo[:, j, w], mh, start=False, stop=k == DC - 1, skip_group_check=True)
                        if k == DC - 1:
                            ins.then_inc(mm_done, 1)

            def ffn_up(g, p, ta=0, tb=0):
                first_pair(g, (x_rhs(ta), x_rhs(tb)), (xl_ready, split_base(p)), t=(ta, tb))
                stat(p, ta)
                for j in range(2, 4):
                    t = tb if j % 2 else ta
                    project(g, j, x_rhs(t), t=t)
                with pe.Fori(1, N_UP) as i:
                    for j in range(4):
                        t = tb if j % 2 else ta
                        project(g + i, j, x_rhs(t), t=t)

            def ffn_down(g, f, t=0):
                def group(i, first=False):
                    for j in range(4):
                        half = j % 2
                        if half == 0:
                            emptied(4 * (g + i) + j - 3)
                        slab(g + i, j, a_rhs(t)[half * HALF:(half + 1) * HALF], W[j - half][:, t:T], start=half == 0,
                             stop=half == 1, each=(al_ready, FC * f + half * HALF, 0) if first and j < 2 else None).then_inc(mm_done, 1)
                group(0, first=True)
                with pe.Fori(1, N_DN) as i:
                    group(i)

            def out_proj(g, rhs, ready, behind=(3, 3, 3, 3)):
                first_pair(g, (rhs, rhs), ready, behind)
                for n in range(2, 4 * N_WO):
                    project(g + n // 4, n % 4, rhs, behind=behind[n] if n < 4 else 3)

            def mm(out, lhsT, rhs, start):
                return pe.matmul(out, lhsT, rhs, start=start, stop=True, skip_group_check=True)

            def turn(out, c, src, b):
                a, e = BLK[b]
                if b < 2:
                    return pe.transpose(out[:, P * c:P * c + P], src[:, a:e], ident)
                return mm(out[0:16, P * c:P * c + P], src[:, a:e], ident, c == 0)

            def forget_logits():
                pe.wait_ge(wffg_ready, DC)
                for k in range(DC):
                    pe.wait_ge(h_landed[k // 2], 16)
                    ins = mm(X[2][0:FOX_H, 0:T], wffg[:, k, :], h[:, k, :], k == 0)
                ins.then_inc(ff_mm, 1)

            def forget_turn():
                pe.wait_ge(ff_step, 3)
                for b, (a, e) in enumerate(BLK):
                    ins = mm(X[2][0:e - a, FOX_H * b:FOX_H * b + FOX_H], ff_s[:, a:e], ident[0:FOX_H, 0:FOX_H], b == 0)
                ins.then_inc(lt_mm, 1)

            def forget_sums():
                pe.wait_ge(lf_ready, 3)
                pe.wait_ge(c1_landed, 16)
                for b, (a, e) in enumerate(BLK):
                    ins = mm(X[2][0:FOX_H, a:T], lf_s[0:e - a, FOX_H * b:FOX_H * b + FOX_H], later[0:e - a, 0:T - a], b == 0)
                ins.then_inc(c_mm, 1)

            def fox_logits(hd):
                c, p0 = hd // 2, 64 * (hd % 2)
                if hd == 0:
                    pe.wait_ge(vt_ready, 3)
                    pe.wait_ge(c_ready, 1)
                else:
                    pe.wait_ge(fl_max, hd)
                pe.wait_ge(evac_done, FK + 2 * c + 1)
                q, k = proj[p0:p0 + 64, FQ + 2 * c, :], proj[p0:p0 + 64, FK + 2 * c, :]

                def bias(out, b, m):
                    return mm(out, ident[0:FOX_H, hd:hd + 1].to_broadcast([FOX_H, m]), csum[:, 0:BLK[b][1]], False)

                mm(X[0][:, 0:128], q[:, 0:128], k[:, 0:128], True)
                mm(X[0][:, 128:384], q[:, 128:256], k[:, 0:256], False)
                bias(X[0][:, 0:128], 0, P)
                bias(X[0][:, 128:384], 1, P)
                mm(X[1][0:16, 0:T], q[:, 256:T], k[:, 0:T], True)
                bias(X[1][0:16, 0:T], 2, 16).then_inc(fl_mm, 1)

            def fox_turn(hd):
                pe.wait_ge(fp_ready, 3 * hd + 3)
                if hd:
                    pe.wait_ge(ft_ready, 2 * hd)
                pb = prob[:, hd % 2, :]
                pe.transpose(X[2][:, 0:128], pb[:, 0:128], ident)
                pe.transpose(X[2][:, 128:256], pb[:, 128:256], ident)
                pe.transpose(X[2][:, 256:272], pb[0:16, 384:512], ident[0:16, 0:16])
                pe.transpose(X[2][:, 272:400], pb[:, 256:384], ident)
                pe.transpose(X[2][:, 400:416], pb[0:16, 512:640], ident[0:16, 0:16])
                mm(X[2][0:16, 416:432], pb[0:16, 640:656], ident[0:16, 0:16], True).then_inc(ft_mm, 1)

            def fox_values(hd):
                c, p0 = hd // 2, 64 * (hd % 2)
                pe.wait_ge(ft_ready, 2 * hd + 2)
                if c and not p0:
                    pe.wait_ge(fo_lo, c)
                for b in range(3):
                    r = BLK[b][1] - BLK[b][0]
                    ins = mm(X[3][p0:p0 + 64, BLK[b][0]:T], vT[0:r, b, 64 * hd:64 * hd + 64],
                             probT[0:r, SB_AT[b]:SB_AT[b] + T - BLK[b][0]], b == 0)
                ins.then_inc(fo_mm, 1)

            def ret_scores(hd):
                pe.wait_ge(rot_ready, 4)
                if hd == 0:
                    pe.wait_ge(fl_max, FOX_H)
                else:
                    pe.wait_ge(rs_ready, 3 * hd)
                if hd == 2:
                    pe.wait_ge(vt_ready, 6)
                p0 = 32 * hd
                for b in range(3):
                    a, e = BLK[b]
                    w = T - RET_FROM[b]
                    at = RET_AT[b] - (RET_AT[1] if b else 0)
                    for half in range(2):
                        ins = mm(X[min(b, 1)][0:e - a, at:at + w], proj[p0:p0 + 32, ROTK + half, a:e],
                                 proj[p0:p0 + 32, ROTQ + half, RET_FROM[b]:T], b < 2 and half == 0)
                ins.then_inc(rs_mm, 1)

            def ret_values(hd):
                pe.wait_ge(rs_ready, 3 * hd + 3)
                if hd == 0:
                    pe.wait_ge(vt_ready, 6)
                else:
                    pe.wait_ge(ro_sq, hd)
                for b in range(3):
                    r = BLK[b][1] - BLK[b][0]
                    ins = mm(X[2][:, RET_FROM[b]:T], vT[0:r, b, P * hd:P * hd + P],
                             decay[0:r, hd % 2, RET_AT[b]:RET_AT[b] + T - RET_FROM[b]], b == 0)
                ins.then_inc(ro_mm, 1)

            def ret_sums(hd):
                pe.wait_ge(ro_sq, hd + 1)
                if hd:
                    pe.wait_ge(rvar_ready, hd)
                mm(X[3][:, 0:T], ones, sq[:, hd % 2, :], True).then_inc(rv_mm, 1)

            def keep_warm(n):
                for _ in range(n):
                    mm(X[0][:, 0:T], vT[:, 0, 0:P], vT[:, 0, 0:T], True)

            pe.wait_ge(warm_set, 1)
            keep_warm(WARM_UP)
            for s in range(4 * N_QKV1):
                project(s // 4, s % 4, X_RHS, each=(xl_ready, 0, 0) if s == 0 else None)
                if s == 2:
                    pe.wait_ge(cst_landed, 16)
                    stat(0)
                    forget_logits()
                if s == 4:
                    forget_turn()
                if s == 5:
                    pe.wait_ge(evac_done, FV + CC)
                    for b, bank in enumerate((0, 1, 3)):
                        for c in range(CC):
                            ins = turn(X[bank], c, proj[:, FV + c, :], b)
                        ins.then_inc(vt_mm, 1)
                if s == FOX_FROM - 1:
                    forget_sums()
                hd = s - FOX_FROM
                if 0 <= hd < FOX_H:
                    fox_logits(hd)
                if 0 <= hd - 3 < FOX_H:
                    fox_values(hd - 3)
                if 0 <= hd - 2 < FOX_H:
                    fox_turn(hd - 2)
                if s == RET_T:
                    pe.wait_ge(evac_done, RV + CC)
                    pe.wait_ge(ft_ready, 2 * FOX_H)
                    pe.wait_ge(fo_lo, CC)
                    pe.wait_ge(rs_ready, 6)
                    for b, bank in enumerate((2, 3, 0)):
                        for c in range(CC):
                            ins = turn(X[bank], c, proj[:, RV + c, :], b)
                        ins.then_inc(vt_mm, 1)
                if RET_S <= s < RET_S + 2:
                    ret_scores(s - RET_S)
                if s >= RET_V:
                    ret_values(s - RET_V)
                if RET_V <= s < RET_V + 2:
                    ret_scores(s - RET_V + 2)
                if s > RET_V:
                    ret_sums(s - RET_V - 1)
            ret_sums(3)
            fox, ret = a_rhs(T_A)[CC:DC], a_rhs(T_A)[0:CC]
            for j in range(4):
                emptied(4 * G_WO1 + j - 3)
                slab(G_WO1, j, fox, W[j][:, T_A:T], stop=False)
            for j in range(4):
                slab(G_WO1, j, ret, W[j][:, T_A:T], at=CC, start=False,
                     each=(ro_lo, 0, 0) if j == 0 else None).then_inc(mm_done, 1)
            for j in range(4):
                project(G_WO1 + 1, j, fox + ret, t=T_A)
            ffn_up(G_UP1, 1, T_A, T_B)
            ffn_down(G_DN1, 0, T_B)
            stat(2, T_B)
            keep_warm(COOL)

            def mixer(g, l):
                def scores(hd):
                    c, p0, bank = hd // 2, 64 * (hd % 2), hd % 2
                    pe.wait_ge(evac_done, 4 * g + G_V + 2 * c + 2)
                    if hd == 1:
                        pe.wait_ge(v2_ready, 3 * l + 1)
                    elif hd >= 2:
                        pe.wait_ge(arg_ready, SB_H * l + hd - 1)
                    for b in range(3):
                        a, w = P * b, T - P * b
                        ins = mm(X[bank][:, SB_AT[b]:SB_AT[b] + w], kpad[p0:p0 + 64, c, a:a + P],
                                 proj[p0:p0 + 64, QQ + c, a:T], b == 0)
                    ins.then_inc(z_mm, 1)

                def sums(hd):
                    bank = hd % 2
                    pe.wait_ge(keep_ready, SB_H * l + hd + 1)
                    for b in range(3):
                        for jb in range(b, 3):
                            r = BLK[jb][1] - BLK[jb][0]
                            w = T - P * jb
                            ins = mm(X[bank][:, SB_AT[b] + P * (jb - b):SB_AT[b] + P * (jb - b) + w],
                                     (trige if jb == b else ones)[0:r, :], keep[0:r, SB_AT[jb]:SB_AT[jb] + w], False)
                    ins.then_inc(cum_mm, 1)

                def values(hd):
                    c, p0 = hd // 2, 64 * (hd % 2)
                    pe.wait_ge(attn_ready, SB_H * l + hd + 1)
                    if hd == 0:
                        pe.wait_ge(v2_ready, 3 * l + 3)
                    elif p0 == 0:
                        pe.wait_ge(o_lo, CC * l + c)
                    for b in range(3):
                        r = BLK[b][1] - BLK[b][0]
                        ins = mm(X[2][p0:p0 + 64, P * b:T], vT[0:r, b, 64 * hd:64 * hd + 64],
                                 attn[0:r, SB_AT[b]:SB_AT[b] + T - P * b], b == 0)
                    ins.then_inc(o_mm, 1)

                def channel_sums(k):
                    pe.wait_ge(ln_sum, 2 * l + k)
                    mm(X[3][:, 0:T], ones, acc[:, :], True).then_inc(ln_mm, 1)

                def branch(ga, j, rhs):
                    emptied(4 * ga + j - 1)
                    for half in range(2):
                        ins = slab(ga, j, rhs, W[(2 * j + half) % 4][:, 0:T], at=CC * half)
                    ins.then_inc(mm_done, 1)

                first_pair(g, (X_RHS, X_RHS), (xl_ready, split_base(4 + 3 * l)))
                stat(4 + 3 * l)
                for s in range(2, 4 * N_MIX):
                    project(g + s // 4, s % 4, X_RHS)
                    if s == G_V + 2:
                        pe.wait_ge(evac_done, 4 * g + G_V)
                        for b in range(3):
                            for c in range(CC):
                                ins = turn(X[1 + b], c, proj[:, VV + c, :], b)
                            ins.then_inc(v2_mm, 1)
                    hd, late = divmod(s - SB_FROM, 2)
                    if not late and 2 <= hd < SB_H + 2:
                        values(hd - 2)
                    if not late and 1 <= hd < SB_H + 1:
                        sums(hd - 1)
                    if not late and 0 <= hd < SB_H:
                        scores(hd)
                    if s == LN_FROM + 1:
                        channel_sums(1)
                    if s == LN_FROM + 5:
                        channel_sums(2)
                ga = g + N_MIX
                pe.wait_ge(o_lo, CC * l + CC)
                for j in range(4):
                    branch(ga, j, A_RHS[0:CC])
                pe.wait_ge(s_lo, CC * l + CC)
                for j in range(4):
                    branch(ga + 1, j, A_RHS[CC:2 * CC])
                out_proj(ga + N_AC, A_RHS[DC:2 * DC], (mix_lo, DC * l), behind=(1, 2, 2, 3))

            with pe.Fori(0, LAYERS) as l:
                g, p = G_LAYER + PER_LAYER * l, 4 + 3 * l
                ffn_up(g + L_UPA, p - 1)
                ffn_down(g + L_DNA, 1 + 2 * l)
                mixer(g + L_MIX, l)
                ffn_up(g + L_UPB, p + 1)
                ffn_down(g + L_DNB, 2 + 2 * l)
            stat(3 + 3 * LAYERS)


def tiles(w, cols):
    k = w.shape[0] // P
    return w[:, cols].reshape(k, P, P).transpose(1, 0, 2).reshape(P, k * P)


def chunk_cols(start, n):
    return [np.arange(start + P * c, start + P * c + P) for c in range(n)]


def interleaved(a, b):
    return [x for pair in zip(a, b) for x in pair]


def half_heads(start):
    head = np.arange(RET_H)[:, None] * RET_DK + np.arange(RET_DK // 2)[None, :]
    return [start + head.reshape(-1), start + RET_DK // 2 + head.reshape(-1)]


def down_slabs(w):
    return [tiles(w[half * HALF * P:(half + 1) * HALF * P], c) for c in chunk_cols(0, DC) for half in range(2)]


def branch_slabs(w):
    cols = chunk_cols(0, DC)
    return [np.concatenate([tiles(w, cols[2 * j]), tiles(w, cols[2 * j + 1])], 1) for j in range(4)]


def chunked(v):
    return np.asarray(v).reshape(-1, P).T


def constants():
    i = np.arange(P)
    ident = np.eye(P)
    trige = (i[:, None] >= i[None, :])
    unseen = np.ones((P, SBW))
    for b, (a, e) in enumerate(BLK):
        key, query = P * b + i[:, None], np.arange(P * b, T)[None, :]
        unseen[:, SB_AT[b]:SB_AT[b] + T - P * b] = ~((key < query) & (key < T))
    every = np.concatenate([np.ones((P, P)), ident, trige, unseen], 1)
    later = (i[:, None] <= np.arange(T)[None, :])
    mask = np.zeros((P, FOXW))
    for b, (a, e) in enumerate(BLK):
        w = FOX_AT[b + 1] - FOX_AT[b] if b < 2 else T
        mask[:, FOX_AT[b]:FOX_AT[b] + w] = np.where(np.arange(w)[None, :] <= a + i[:, None], 0.0, NEG * FOX_DH ** 0.5)
    dist = np.full((P, RETW), 1e5)
    for b, (a, e) in enumerate(BLK):
        s, t = a + i[:, None], np.arange(RET_FROM[b], T)[None, :]
        seen = ((s + PAD) // CHUNK <= (t + PAD) // CHUNK) & (s < T)
        dist[:, RET_AT[b]:RET_AT[b] + T - RET_FROM[b]] = np.where(seen, np.abs(t - s), 1e5)
    half = RET_DK // 2
    inv = 1.0 / (np.float32(10000.0) ** (np.arange(half, dtype=np.float32) / np.float32(half)))
    ang = (np.arange(T, dtype=np.float32)[None, :] + np.float32(PAD)) * inv.astype(np.float32)[:, None]
    ang = np.tile(ang, (RET_H, 1)).astype(np.float32)
    first = np.concatenate([later, mask, dist, np.cos(ang), np.sin(ang)], 1)
    return first.astype(np.float32), every.astype(np.float32)


def kernel(**inputs):
    import concourse.bacc as bacc
    from concourse.bass_utils import run_bass_kernel_spmd

    a = {k: np.asarray(v) for k, v in inputs.items()}
    w_in = a["w_in"][0]
    at = np.cumsum([0, 256, 256, 512, 512, 512, 512, 512])
    order = chunk_cols(at[6], CC) + interleaved(chunk_cols(at[4], CC), chunk_cols(at[5], CC)) + half_heads(at[0]) + half_heads(at[1]) + chunk_cols(at[2], 8)
    s8 = [tiles(w_in, c) for c in order]
    w_out = np.roll(a["w_out"][0], D // 2, axis=0)
    s8 += [tiles(w_out, c) for c in chunk_cols(0, DC)]
    s8 += [tiles(a["w_up"][0], c) for c in interleaved(chunk_cols(0, FC), chunk_cols(FF, FC))]
    s11 = down_slabs(a["w_down"][0])
    for l in range(LAYERS):
        for f in ("ffn1", "ffn2"):
            up = [tiles(w, c) for c in chunk_cols(0, FC) for w in (a[f + "_w_gate_2"][l], a[f + "_w_up_2"][l])]
            if f == "ffn2":
                w = a["w_in_2"][l]
                cols = (interleaved(chunk_cols(1536, 4), chunk_cols(2048, 4)) + chunk_cols(1024, 4)
                        + interleaved(chunk_cols(0, 4), chunk_cols(512, 4)) + chunk_cols(2560, 16))
                s8 += [tiles(w, c) for c in cols]
                s8 += branch_slabs(a["w_attn_out_2"][l]) + branch_slabs(a["w_conv_out_2"][l])
                s8 += [tiles(a["w_out_2"][l], c) for c in chunk_cols(0, DC)]
            s8 += up
            s11 += down_slabs(a[f + "_w_down_2"][l])
    s8 += s8[:4]
    gains = [a["attn_norm_g"][0], a["ffn_norm_g"][0], a["final_norm_g"]]
    for l in range(LAYERS):
        gains += [a["ffn1_norm_2"][l], a["mix_norm_2"][l], a["ffn2_norm_2"][l]]
    gains.append(a["final_norm_2"])
    prm = [chunked(g) for g in gains] + [chunked(a["ret_norm_g"][0])]
    prm.append(a["conv_w"][0].reshape(CONV_W, FC, P).transpose(2, 1, 0).reshape(P, FC * CONV_W))
    prm.append(chunked(a["conv_b"][0]))
    prm += [a["conv_w_2"][l].reshape(CONV_K, CC, P).transpose(2, 1, 0).reshape(P, CC * CONV_K) for l in range(LAYERS)]
    prm += [chunked(a[n]) for n in ("conv_b_2", "conv_ln_g_2", "conv_ln_b_2")]
    first, every = constants()
    arrays = {
        "hT": np.concatenate([a["meta_tokens"], a["x"][0]], 0).T.reshape(DC, P, T).transpose(1, 0, 2),
        "meta2": a["meta_2"].T.reshape(DC, P, META).transpose(1, 0, 2),
        "w8": np.stack(s8),
        "w11": np.stack(s11),
        "wff": w_in[:, at[7]:].reshape(DC, P, 8).transpose(1, 0, 2),
        "fbias": a["fox_forget_b"].reshape(FOX_H, 1),
        "prm": np.concatenate(prm, 1),
        "cst1": first,
        "cst": every,
    }
    arrays = {k: np.ascontiguousarray(v) for k, v in arrays.items()}

    nc = bacc.Bacc("TRN2", target_bir_lowering=False, num_devices=1)
    args = [nc.dram_tensor("in_" + k, v.shape, mybir.dt.from_np(v.dtype), kind="ExternalInput").ap()
            for k, v in arrays.items()]
    out = nc.dram_tensor("out_0", (P, DC, SEQ), F32, kind="ExternalOutput").ap()
    build(nc, *args, out)
    r = run_bass_kernel_spmd(nc, [{"in_" + k: v for k, v in arrays.items()}], core_ids=[0])
    got = r.results[0]["out_0"]
    return got.transpose(2, 1, 0).reshape(1, SEQ, D)
```
